# Optimizing a Trainium2 kernel written in Bass

```python
import math
import jax, jax.numpy as jnp
from jax import lax
import numpy as np

D_MODEL = 1024
BATCH = 1
SEQ = 256
DEPTH = 2

N_A_LAYERS = DEPTH // 2
N_B_LAYERS = DEPTH - N_A_LAYERS
HEAD_DIM = 64
N_HEADS = D_MODEL // (2 * HEAD_DIM)
D_FF = 2816
CONV_WIDTH = 3
Q_BLOCK = 128
NORM_EPS = 1e-6


def rmsnorm(x, g):
    xf = x.astype(jnp.float32)
    y = xf * lax.rsqrt(jnp.mean(xf * xf, axis=-1, keepdims=True) + NORM_EPS)
    return (y * g.astype(jnp.float32)).astype(x.dtype)

def swiglu(x, w_gu, w_down):
    gate, up = jnp.split(x @ w_gu, 2, axis=-1)
    return (jax.nn.silu(gate) * up) @ w_down

def short_gated_conv(xn, w_in, conv_k, w_out):
    b_gate, c_gate, z = jnp.split(xn @ w_in, 3, axis=-1)
    u = c_gate * z
    rhs = conv_k[:, None, :].astype(u.dtype)
    conv = lax.conv_general_dilated(
        u, rhs, window_strides=(1,), padding=[(CONV_WIDTH - 1, 0)],
        dimension_numbers=('NWC', 'WIO', 'NWC'), feature_group_count=u.shape[-1])
    return (b_gate * conv) @ w_out

def alibi_slopes(n_heads):
    return 2.0 ** (-8.0 * jnp.arange(1, n_heads + 1, dtype=jnp.float32) / n_heads)

def shared_kv(h, kv_norm_g, w_kv):
    Bsz, S, _ = h.shape
    k_flat, v_flat = jnp.split(rmsnorm(h, kv_norm_g) @ w_kv, 2, axis=-1)
    k = k_flat.reshape(Bsz, S, N_HEADS, 2, HEAD_DIM)
    v = v_flat.reshape(Bsz, S, N_HEADS, 2 * HEAD_DIM)
    return k, v

def diff_attention(xn, k, v, w_q, lam_params, subln_g, w_o, lambda_init):
    Bsz, S, _ = xn.shape
    q = (xn @ w_q).reshape(Bsz, S, N_HEADS, 2, HEAD_DIM)
    lp = lam_params.astype(jnp.float32)
    lam = jnp.exp(jnp.sum(lp[0] * lp[1])) - jnp.exp(jnp.sum(lp[2] * lp[3])) + lambda_init
    scale = HEAD_DIM ** -0.5
    n_blocks = S // Q_BLOCK
    q_blocks = q.reshape(Bsz, n_blocks, Q_BLOCK, N_HEADS, 2, HEAD_DIM).swapaxes(0, 1)
    slopes = alibi_slopes(N_HEADS)
    kpos = jnp.arange(S)

    def one_block(args):
        q_blk, start = args
        qpos = start + jnp.arange(Q_BLOCK)
        dist = (qpos[:, None] - kpos[None, :]).astype(jnp.float32)
        s = jnp.einsum('bqhcd,bkhcd->bhcqk', q_blk, k,
                       preferred_element_type=jnp.float32) * scale
        s = s - slopes[None, :, None, None, None] * dist
        s = jnp.where(dist >= 0, s, -jnp.inf)
        p = jax.nn.softmax(s, axis=-1)
        a = p[:, :, 0] - lam * p[:, :, 1]
        return jnp.einsum('bhqk,bkhe->bqhe', a, v)

    o = lax.map(one_block, (q_blocks, jnp.arange(n_blocks) * Q_BLOCK))
    o = o.swapaxes(0, 1).reshape(Bsz, S, N_HEADS, 2 * HEAD_DIM).astype(jnp.float32)
    o = o * lax.rsqrt(jnp.mean(o * o, axis=-1, keepdims=True) + NORM_EPS)
    o = o * subln_g.astype(jnp.float32) * (1.0 - lambda_init)
    return o.reshape(Bsz, S, N_HEADS * 2 * HEAD_DIM).astype(xn.dtype) @ w_o

def first_inputs(seed: int = 0) -> dict:
    key = jax.random.key(seed)
    ks = jax.random.split(key, 16)
    D = D_MODEL
    nrm = lambda k, shape, fan_in: jax.random.normal(k, shape, jnp.float32) * fan_in ** -0.5
    x = jax.random.normal(ks[0], (BATCH, SEQ, D), jnp.float32)
    ffn_w_gu = nrm(ks[1], (DEPTH, 2, D, 2 * D_FF), D)
    ffn_w_down = nrm(ks[2], (DEPTH, 2, D_FF, D), D_FF)
    norm_g = 1.0 + 0.05 * jax.random.normal(ks[3], (DEPTH, 6, D), jnp.float32)
    conv_w_in = nrm(ks[4], (N_A_LAYERS, D, 3 * D), D)
    conv_k = nrm(ks[5], (N_A_LAYERS, CONV_WIDTH, D), CONV_WIDTH)
    conv_w_out = nrm(ks[6], (N_A_LAYERS, D, D), D)
    kv_norm_g = 1.0 + 0.05 * jax.random.normal(ks[7], (D,), jnp.float32)
    w_kv = nrm(ks[8], (D, 2 * D), D)
    attn_w_q = nrm(ks[9], (N_B_LAYERS, D, D), D)
    attn_lambda = 0.1 * jax.random.normal(ks[10], (N_B_LAYERS, 4, HEAD_DIM), jnp.float32)
    attn_subln_g = 1.0 + 0.05 * jax.random.normal(ks[11], (N_B_LAYERS, 2 * HEAD_DIM), jnp.float32)
    attn_w_o = nrm(ks[12], (N_B_LAYERS, D, D), D)
    return {"x": x, "ffn_w_gu": ffn_w_gu, "ffn_w_down": ffn_w_down, "norm_g": norm_g,
            "conv_w_in": conv_w_in, "conv_k": conv_k, "conv_w_out": conv_w_out,
            "kv_norm_g": kv_norm_g, "w_kv": w_kv, "attn_w_q": attn_w_q,
            "attn_lambda": attn_lambda, "attn_subln_g": attn_subln_g, "attn_w_o": attn_w_o}

def first_block(x, ffn_w_gu, ffn_w_down, norm_g, conv_w_in, conv_k, conv_w_out,
              kv_norm_g, w_kv, attn_w_q, attn_lambda, attn_subln_g, attn_w_o):
    h = x
    k = v = None
    for l in range(DEPTH):
        g = norm_g[l]
        if l == N_A_LAYERS:
            k, v = shared_kv(h, kv_norm_g, w_kv)
        h = h + 0.5 * rmsnorm(swiglu(rmsnorm(h, g[0]), ffn_w_gu[l, 0], ffn_w_down[l, 0]), g[1])
        xn = rmsnorm(h, g[2])
        if l < N_A_LAYERS:
            mix = short_gated_conv(xn, conv_w_in[l], conv_k[l], conv_w_out[l])
        else:
            j = l - N_A_LAYERS
            lambda_init = 0.8 - 0.6 * math.exp(-0.3 * l)
            mix = diff_attention(xn, k, v, attn_w_q[j], attn_lambda[j],
                                 attn_subln_g[j], attn_w_o[j], lambda_init)
        h = h + rmsnorm(mix, g[3])
        h = h + 0.5 * rmsnorm(swiglu(rmsnorm(h, g[4]), ffn_w_gu[l, 1], ffn_w_down[l, 1]), g[5])
    return h


DEPTH_2 = 1

CHUNK = 64
EPS = 1e-6
N_HEADS_2 = 16
N_KV_HEADS = 4
ROPE_DIM = HEAD_DIM // 4
ROPE_THETA = 500000.0
IDX_HEADS = 8
IDX_DIM = 64
TOPK_MAX = 256
SSD_D_INNER = 2 * D_MODEL
SSD_HEAD_DIM = 64
SSD_HEADS = SSD_D_INNER // SSD_HEAD_DIM
SSD_GROUPS = 4
SSD_STATE = 128
SSD_CONV = 4
SSD_XBC = SSD_D_INNER + 2 * SSD_GROUPS * SSD_STATE
N_EXPERT_GROUPS = 4
EXPERTS_PER_GROUP = 8
EXPERT_TOPK = 2
EXPERT_HIDDEN = 256
Q_W = N_HEADS_2 * HEAD_DIM
KV_W = N_KV_HEADS * HEAD_DIM
IQ_W = IDX_HEADS * IDX_DIM
SPLITS = (Q_W, KV_W, KV_W, IQ_W, IDX_DIM, IDX_HEADS, SSD_D_INNER, SSD_XBC, SSD_HEADS, D_MODEL, D_MODEL)
IN_PROJ_W = sum(SPLITS)


def rmsnorm_2(x, g):
    xf = x.astype(jnp.float32)
    y = xf * lax.rsqrt(jnp.mean(xf * xf, axis=-1, keepdims=True) + EPS)
    return (y * g.astype(jnp.float32)).astype(x.dtype)

def rope_partial(x, pos):
    half = ROPE_DIM // 2
    inv = ROPE_THETA ** (-jnp.arange(half, dtype=jnp.float32) * 2.0 / ROPE_DIM)
    ang = pos.astype(jnp.float32)[:, None] * inv[None, :]
    cos = jnp.cos(ang)[:, None, :]
    sin = jnp.sin(ang)[:, None, :]
    xr = x[..., :ROPE_DIM].astype(jnp.float32)
    x1, x2 = xr[..., :half], xr[..., half:]
    rot = jnp.concatenate([x1 * cos - x2 * sin, x2 * cos + x1 * sin], axis=-1)
    return jnp.concatenate([rot.astype(x.dtype), x[..., ROPE_DIM:]], axis=-1)

def dsa_attention(q, k, v, iq, ik, iw):
    Bsz, T = q.shape[0], q.shape[1]
    topk = min(TOPK_MAX, T // 4)
    nblk = T // Q_BLOCK
    grp = N_HEADS_2 // N_KV_HEADS
    key_chunk = jnp.arange(T) // CHUNK
    ikf = ik.astype(jnp.float32)

    def to_blocks(a):
        return a.reshape(Bsz, nblk, Q_BLOCK, *a.shape[2:]).swapaxes(0, 1)

    def one_block(args):
        qb, iqb, iwb, start = args
        q_chunk = (start + jnp.arange(Q_BLOCK)) // CHUNK
        admissible = key_chunk[None, :] <= q_chunk[:, None]
        rel = jax.nn.relu(jnp.einsum('bqhd,bsd->bqhs', iqb.astype(jnp.float32), ikf) * IDX_DIM ** -0.5)
        score = jnp.einsum('bqhs,bqh->bqs', rel, iwb.astype(jnp.float32) * IDX_HEADS ** -0.5)
        score = jnp.where(admissible[None], score, -jnp.inf)
        top_s, sel = lax.top_k(score, topk)
        valid = jnp.isfinite(top_s)
        k_sel = jax.vmap(lambda kk, ii: kk[ii])(k, sel)
        v_sel = jax.vmap(lambda vv, ii: vv[ii])(v, sel)
        qg = qb.reshape(Bsz, Q_BLOCK, N_KV_HEADS, grp, HEAD_DIM).astype(jnp.float32)
        logits = jnp.einsum('bqhgd,bqkhd->bqhgk', qg, k_sel.astype(jnp.float32)) * HEAD_DIM ** -0.5
        logits = jnp.where(valid[:, :, None, None, :], logits, -jnp.inf)
        p = jax.nn.softmax(logits, axis=-1)
        o = jnp.einsum('bqhgk,bqkhd->bqhgd', p, v_sel.astype(jnp.float32))
        return o.reshape(Bsz, Q_BLOCK, N_HEADS_2 * HEAD_DIM).astype(q.dtype)

    starts = jnp.arange(nblk, dtype=jnp.int32) * Q_BLOCK
    out = lax.map(one_block, (to_blocks(q), to_blocks(iq), to_blocks(iw), starts))
    return out.swapaxes(0, 1).reshape(Bsz, T, N_HEADS_2 * HEAD_DIM)

def causal_depthwise_conv(x, w, b):
    y = lax.conv_general_dilated(x, w[:, None, :], window_strides=(1,),
                                 padding=[(w.shape[0] - 1, 0)],
                                 dimension_numbers=('NWC', 'WIO', 'NWC'),
                                 feature_group_count=x.shape[-1])
    return y + b

def ssd_chunked(xh, dt, A, Bm, Cm):
    Bsz, T, H, P = xh.shape
    nc = T // CHUNK
    R = H // SSD_GROUPS
    x = (xh * dt[..., None]).reshape(Bsz, nc, CHUNK, SSD_GROUPS, R, P)
    a_cs = jnp.cumsum((dt * A).reshape(Bsz, nc, CHUNK, SSD_GROUPS, R), axis=2)
    Bc = Bm.reshape(Bsz, nc, CHUNK, SSD_GROUPS, SSD_STATE)
    Cc = Cm.reshape(Bsz, nc, CHUNK, SSD_GROUPS, SSD_STATE)
    seg = a_cs[:, :, :, None] - a_cs[:, :, None, :]
    causal = jnp.tril(jnp.ones((CHUNK, CHUNK), dtype=bool))[None, None, :, :, None, None]
    decay = jnp.exp(jnp.where(causal, seg, -jnp.inf))
    cb = jnp.einsum('bclgn,bcsgn->bclsg', Cc, Bc)
    y_diag = jnp.einsum('bclsg,bclsgr,bcsgrp->bclgrp', cb, decay, x)
    decay_to_end = jnp.exp(a_cs[:, :, -1:] - a_cs)
    states = jnp.einsum('bclgn,bclgr,bclgrp->bcgrpn', Bc, decay_to_end, x)
    chunk_decay = jnp.exp(a_cs[:, :, -1])

    def step(h, inp):
        dec, st = inp
        return dec[..., None, None] * h + st, h

    h0 = jnp.zeros((Bsz, SSD_GROUPS, R, P, SSD_STATE), jnp.float32)
    _, prev = lax.scan(step, h0, (chunk_decay.swapaxes(0, 1), states.swapaxes(0, 1)))
    prev = prev.swapaxes(0, 1)
    y_off = jnp.einsum('bclgn,bcgrpn,bclgr->bclgrp', Cc, prev, jnp.exp(a_cs))
    return (y_diag + y_off).reshape(Bsz, T, H, P)

def gated_group_rmsnorm(y, z, g):
    yf = y.astype(jnp.float32) * jax.nn.silu(z.astype(jnp.float32))
    yg = yf.reshape(*yf.shape[:-1], SSD_GROUPS, -1)
    yg = yg * lax.rsqrt(jnp.mean(yg * yg, axis=-1, keepdims=True) + EPS)
    return yg.reshape(yf.shape) * g.astype(jnp.float32)

def hier_moe(h, w_rg, b_rg, w_re, b_re, w_gate, w_up, w_down):
    Bsz, T, D = h.shape
    hf = h.reshape(-1, D)
    g_logits = (hf @ w_rg + b_rg).astype(jnp.float32)
    g_prob = jax.nn.softmax(g_logits, axis=-1)
    g_idx = jnp.argmax(g_logits, axis=-1)
    g_w = jnp.take_along_axis(g_prob, g_idx[:, None], axis=-1)
    e_logits = (hf @ w_re + b_re).astype(jnp.float32).reshape(-1, N_EXPERT_GROUPS, EXPERTS_PER_GROUP)
    e_in = jnp.take_along_axis(e_logits, g_idx[:, None, None], axis=1)[:, 0]
    top_v, top_i = lax.top_k(e_in, EXPERT_TOPK)
    top_p = jax.nn.softmax(top_v, axis=-1)
    within = jnp.sum(jax.nn.one_hot(top_i, EXPERTS_PER_GROUP, dtype=jnp.float32) * top_p[..., None], axis=1)
    combine = jax.nn.one_hot(g_idx, N_EXPERT_GROUPS, dtype=jnp.float32)[:, :, None] * (g_w * within)[:, None, :]
    combine = combine.astype(hf.dtype)
    out = jnp.zeros_like(hf)
    for g in range(N_EXPERT_GROUPS):
        a = jnp.einsum('nd,edf->nef', hf, w_gate[g])
        u = jnp.einsum('nd,edf->nef', hf, w_up[g])
        act = jax.nn.silu(a) * u * combine[:, g, :, None]
        out = out + jnp.einsum('nef,efd->nd', act, w_down[g])
    return out.reshape(Bsz, T, D)

def second_inputs(seed: int = 0) -> dict:
    key = jax.random.key(seed)
    ks = jax.random.split(key, 24)
    L = DEPTH_2
    f32 = jnp.float32

    def nrm(k, shape, scale):
        return jax.random.normal(k, shape, f32) * scale

    def gain(k, n):
        return 1.0 + 0.02 * jax.random.normal(k, (L, n), f32)

    dt0 = jnp.exp(jax.random.uniform(ks[8], (L, SSD_HEADS), f32, math.log(1e-3), math.log(1e-1)))
    return {
        "x": nrm(ks[0], (BATCH, SEQ, D_MODEL), 1.0),
        "attn_norm": gain(ks[1], D_MODEL),
        "w_in": nrm(ks[2], (L, D_MODEL, IN_PROJ_W), D_MODEL ** -0.5),
        "q_norm": gain(ks[3], HEAD_DIM),
        "k_norm": gain(ks[4], HEAD_DIM),
        "idx_k_norm": gain(ks[5], IDX_DIM),
        "conv_w": nrm(ks[6], (L, SSD_CONV, SSD_XBC), SSD_CONV ** -0.5),
        "conv_b": nrm(ks[7], (L, SSD_XBC), 0.02),
        "dt_bias": dt0 + jnp.log(-jnp.expm1(-dt0)),
        "a_log": jnp.log(jax.random.uniform(ks[9], (L, SSD_HEADS), f32, 1.0, 16.0)),
        "d_skip": 1.0 + 0.1 * jax.random.normal(ks[10], (L, SSD_HEADS), f32),
        "ssd_norm": gain(ks[11], SSD_D_INNER),
        "w_attn_branch": nrm(ks[12], (L, Q_W, D_MODEL), Q_W ** -0.5),
        "w_ssd_branch": nrm(ks[13], (L, SSD_D_INNER, D_MODEL), SSD_D_INNER ** -0.5),
        "w_out": nrm(ks[14], (L, D_MODEL, D_MODEL), D_MODEL ** -0.5),
        "ffn_norm": gain(ks[15], D_MODEL),
        "w_route_group": nrm(ks[16], (L, D_MODEL, N_EXPERT_GROUPS), D_MODEL ** -0.5),
        "b_route_group": nrm(ks[17], (L, N_EXPERT_GROUPS), 0.01),
        "w_route_expert": nrm(ks[18], (L, D_MODEL, N_EXPERT_GROUPS * EXPERTS_PER_GROUP), D_MODEL ** -0.5),
        "b_route_expert": nrm(ks[19], (L, N_EXPERT_GROUPS * EXPERTS_PER_GROUP), 0.01),
        "w_gate": nrm(ks[20], (L, N_EXPERT_GROUPS, EXPERTS_PER_GROUP, D_MODEL, EXPERT_HIDDEN), D_MODEL ** -0.5),
        "w_up": nrm(ks[21], (L, N_EXPERT_GROUPS, EXPERTS_PER_GROUP, D_MODEL, EXPERT_HIDDEN), D_MODEL ** -0.5),
        "w_down": nrm(ks[22], (L, N_EXPERT_GROUPS, EXPERTS_PER_GROUP, EXPERT_HIDDEN, D_MODEL), EXPERT_HIDDEN ** -0.5),
    }

def second_block(x, attn_norm, w_in, q_norm, k_norm, idx_k_norm, conv_w, conv_b, dt_bias, a_log, d_skip,
              ssd_norm, w_attn_branch, w_ssd_branch, w_out, ffn_norm, w_route_group, b_route_group,
              w_route_expert, b_route_expert, w_gate, w_up, w_down):
    Bsz, T, _ = x.shape
    pos = jnp.arange(T)
    offs = np.cumsum(SPLITS)[:-1].tolist()
    for l in range(DEPTH_2):
        h = rmsnorm_2(x, attn_norm[l])
        proj = h @ w_in[l]
        (q, k, v, iq, ik, iw, z, xbc, dt_raw, gate_a, gate_b) = jnp.split(proj, offs, axis=-1)
        q = rope_partial(rmsnorm_2(q.reshape(Bsz, T, N_HEADS_2, HEAD_DIM), q_norm[l]), pos)
        k = rope_partial(rmsnorm_2(k.reshape(Bsz, T, N_KV_HEADS, HEAD_DIM), k_norm[l]), pos)
        v = v.reshape(Bsz, T, N_KV_HEADS, HEAD_DIM)
        iq = rope_partial(iq.reshape(Bsz, T, IDX_HEADS, IDX_DIM), pos)
        ik = rope_partial(rmsnorm_2(ik, idx_k_norm[l])[:, :, None, :], pos)[:, :, 0, :]
        y_attn = dsa_attention(q, k, v, iq, ik, iw)
        xbc = jax.nn.silu(causal_depthwise_conv(xbc, conv_w[l], conv_b[l]))
        xs, bs, cs = jnp.split(xbc, [SSD_D_INNER, SSD_D_INNER + SSD_GROUPS * SSD_STATE], axis=-1)
        xh = xs.reshape(Bsz, T, SSD_HEADS, SSD_HEAD_DIM).astype(jnp.float32)
        dt = jax.nn.softplus(dt_raw.astype(jnp.float32) + dt_bias[l].astype(jnp.float32))
        A = -jnp.exp(a_log[l].astype(jnp.float32))
        y_ssd = ssd_chunked(xh, dt, A,
                            bs.reshape(Bsz, T, SSD_GROUPS, SSD_STATE).astype(jnp.float32),
                            cs.reshape(Bsz, T, SSD_GROUPS, SSD_STATE).astype(jnp.float32))
        y_ssd = y_ssd + d_skip[l].astype(jnp.float32)[:, None] * xh
        y_ssd = gated_group_rmsnorm(y_ssd.reshape(Bsz, T, SSD_D_INNER), z, ssd_norm[l]).astype(x.dtype)
        merged = jax.nn.sigmoid(gate_a) * (y_attn @ w_attn_branch[l]) + jax.nn.sigmoid(gate_b) * (y_ssd @ w_ssd_branch[l])
        x = x + merged @ w_out[l]
        x = x + hier_moe(rmsnorm_2(x, ffn_norm[l]), w_route_group[l], b_route_group[l], w_route_expert[l],
                         b_route_expert[l], w_gate[l], w_up[l], w_down[l])
    return x


def setup_inputs(seed=0):
    out = dict(first_inputs(seed))
    for name, value in second_inputs(seed + 1).items():
        if name != "x":
            out[name + "_2"] = value
    return out


def reference(
    x, ffn_w_gu, ffn_w_down, norm_g, conv_w_in, conv_k, conv_w_out, kv_norm_g, w_kv, attn_w_q,
    attn_lambda, attn_subln_g, attn_w_o, attn_norm_2, w_in_2, q_norm_2, k_norm_2, idx_k_norm_2,
    conv_w_2, conv_b_2, dt_bias_2, a_log_2, d_skip_2, ssd_norm_2, w_attn_branch_2,
    w_ssd_branch_2, w_out_2, ffn_norm_2, w_route_group_2, b_route_group_2, w_route_expert_2,
    b_route_expert_2, w_gate_2, w_up_2, w_down_2,
):
    x = first_block(
        x, ffn_w_gu, ffn_w_down, norm_g, conv_w_in, conv_k, conv_w_out, kv_norm_g, w_kv,
        attn_w_q, attn_lambda, attn_subln_g, attn_w_o,
    )
    return second_block(
        x, attn_norm_2, w_in_2, q_norm_2, k_norm_2, idx_k_norm_2, conv_w_2, conv_b_2, dt_bias_2,
        a_log_2, d_skip_2, ssd_norm_2, w_attn_branch_2, w_ssd_branch_2, w_out_2, ffn_norm_2,
        w_route_group_2, b_route_group_2, w_route_expert_2, b_route_expert_2, w_gate_2, w_up_2,
        w_down_2,
    )


_drawn_inputs = setup_inputs


def setup_inputs(seed=0):
    import zlib

    import numpy as np

    out = dict(_drawn_inputs(seed))
    spreads = {}
    factors = {'attn_norm_2': 3.977,
     'q_norm_2': 8.0,
     'k_norm_2': 8.0,
     'idx_k_norm_2': 5.957,
     'conv_b_2': 4.259,
     'ssd_norm_2': 8.0,
     'ffn_norm_2': 4.729,
     'b_route_group_2': 8.0,
     'b_route_expert_2': 7.83,
     'd_skip_2': 8.0}
    for name, (base, spread) in spreads.items():
        noise = np.random.default_rng([zlib.crc32(name.encode()), seed]).standard_normal(out[name].shape)
        drawn = base * np.exp(spread * noise) if base else spread * noise
        out[name] = __import__('jax').numpy.asarray(drawn.astype(out[name].dtype))
    for name, factor in factors.items():
        out[name] = (out[name] * factor).astype(out[name].dtype)
    return out
```

```python
import math
from contextlib import ExitStack

import concourse.bass as bass
from concourse import mybir
import numpy as np

F32, F32R, I32 = mybir.dt.float32, mybir.dt.float32r, mybir.dt.int32
ALU = mybir.AluOpType
ACT = mybir.ActivationFunctionType
X = mybir.AxisListType.X

P = 128
T = 256
NT = T // P
D = 1024
KD = D // P
SLOT = 2048
RING = 3
FF_STEPS = 2816 // 256
EXPERTS = 32
EPS = 1e-6
NEG = -1e30
TAKEN = -3e38
HEADS1, HD = 8, 64
LAMBDA_INIT = 0.8 - 0.6 * math.exp(-0.3)
TOPK = 64
HEADS2, IDX_HEADS = 16, 8
NORMED = 21
ROPED = 29
SSD_HEADS, SSD_P = 32, 64

COLS = {}
_at = 0
for _name, _n in (("g00", 8), ("g02", 8), ("g04", 8), ("g10", 8), ("g12", 8), ("g14", 8), ("kv", 8),
                  ("conv_k", 24), ("subln", 1), ("attn2", 8), ("ffn2", 8), ("ssd", 16),
                  ("conv_w", 96), ("conv_b", 24)):
    COLS[_name] = _at
    _at += _n
N_COLS = _at
C_ID, C_TRI, C_ONE, C_TRI2, C_GT, C_COS, C_SIN, C_W4, C_W32 = 0, 128, 256, 384, 512, 640, 656, 672, 676
N_CONST = 708


class Signal:

    def __init__(self, sem, base=0):
        self.sem, self.base = sem, base

    def at(self, k):
        return self.base + k + 1

    def passed(self, n):
        self.base += n


class Link:

    def __init__(self, sem):
        self.sem, self.count, self.loop = sem, 0, 0

    def __call__(self, eng, ins):
        self.count += 1
        ins.then_inc(self.sem, 1)
        eng.wait_ge(self.sem, self.loop + self.count)


def build(nc, stream, x_in, out, cols, const, attn_const, adm_const, rows, lam_in):
    n_slots = stream.shape[0]
    ctx = ExitStack()
    with ctx:
        def sb(name, shape, dt=F32, where=ctx):
            return where.enter_context(nc.sbuf_tensor(name, shape, dt))

        def signal(name, base=0):
            return Signal(ctx.enter_context(nc.semaphore(name)), base)

        raw = sb("raw", [P, RING, SLOT])
        whi = sb("whi", [P, RING, SLOT], F32R)
        wlo = sb("wlo", [P, RING, SLOT], F32R)
        h = sb("h", [P, NT, D])
        xn = sb("xn", [P, NT, D])
        xh = sb("xh", [P, KD, T], F32R)
        xl = sb("xl", [P, KD, T], F32R)
        gains = sb("gains", [P, 2, D])
        col = sb("col", [P, N_COLS])
        cst = sb("cst", [P, N_CONST])
        zero = sb("zero", [P, 512], F32R)
        ss = sb("ss", [P, 48])
        rs = sb("rs", [P, 48])
        rt = sb("rt", [P, 48])
        dt_raw = sb("dt_raw", [P, NT, 32])
        ident = cst[:, C_ID:C_ID + P]

        A = ctx.enter_context(nc.psum_tensor("A", [P, 4, 512], F32))
        Y = ctx.enter_context(nc.psum_tensor("Y", [P, NT, D], F32))
        Y4 = Y[:, :, :].rearrange("p t (b n) -> p (t b) n", n=512)
        YT = Y[:, :, :].rearrange("p t (k n) -> p (t k) n", n=T)

        raw_loaded = [signal(f"raw_loaded{r}") for r in range(RING)]
        hi_ready = signal("hi_ready")
        lo_ready = signal("lo_ready", RING)
        slot_done = signal("slot_done")
        half_done = signal("half_done")
        group_free = signal("group_free", 1)
        act_free = signal("act_free")
        xt_hi = signal("xt_hi")
        xt_ready = signal("xt_ready")
        xn_ready = signal("xn_ready")
        sq_done = signal("sq_done")
        transposed = signal("transposed")
        silu_ready = signal("silu_ready")
        h_ready = signal("h_ready")
        h_new = signal("h_new")
        c_copied = signal("c_copied")
        u_ready = signal("u_ready")
        s_ready = signal("s_ready")
        m_ready = signal("m_ready")
        e_ready = signal("e_ready")
        a_ready = signal("a_ready")
        at_ready = signal("at_ready")
        at_copied = signal("at_copied")
        o_ready = signal("o_ready")
        side = signal("side")
        ask = signal("ask")
        consts_in = signal("consts_in")
        gain_in = [signal(f"gain_in{i}") for i in range(2)]
        phase_in = [signal("attn_in"), signal("block2_in")]
        zero_ready = signal("zero_ready")
        stored = signal("stored")
        vlink = Link(ctx.enter_context(nc.semaphore("dve_order")))

        block = ctx.enter_context(nc.Block())

        class State:
            slot = 0
            act_split = 0
            dve_split = 0
            norms = 0
            phase = 0
        st = State

        def split_hi(act, n, i=0):
            act.wait_ge(raw_loaded[n % RING].sem, 16 * (n // RING + 1) + 32 * i)
            if n >= RING:
                act.wait_ge(slot_done.sem, n - RING + 1 + 6 * i)
            nc.scalar.activation(whi[:, n % RING, :], raw[:, n % RING, :], ACT.Copy).then_inc(hi_ready.sem, 1)

        def split_lo(dve, n, i=0):
            dve.wait_ge(hi_ready.sem, n + 1 + 6 * i)
            nc.vector.tensor_tensor(wlo[:, n % RING, :], raw[:, n % RING, :],
                                    whi[:, n % RING, :].bitcast(F32), ALU.subtract).then_inc(lo_ready.sem, 1)

        def act_split_upto(act, n):
            while st.act_split <= min(n, n_slots - 1):
                split_hi(act, st.act_split)
                st.act_split += 1

        def dve_split_upto(dve, n):
            while st.dve_split <= min(n, n_slots - 1):
                split_lo(dve, st.dve_split)
                st.dve_split += 1

        def wait_product(eng, t):
            if t == 0:
                eng.wait_ge(half_done.sem, half_done.base)
            else:
                eng.wait_ge(slot_done.sem, st.slot)

        def wait_slot(pe, n, i=0):
            pe.wait_ge(lo_ready.sem, n + 1 + RING + 6 * i)

        def column_slot(pe, n, bank, features_out, width=256, i=0, first=False):
            wait_slot(pe, n, i)
            wh = whi[:, n % RING, :].rearrange("p (k c) -> p k c", k=KD)
            wl = wlo[:, n % RING, :].rearrange("p (k c) -> p k c", k=KD)
            for m in range(2):
                o = slice(m * P, (m + 1) * P)
                for k in range(KD):
                    if first and m == 0:
                        pe.wait_ge(xt_ready.sem, xt_ready.base - KD + max(k, 1) + 1)
                    if features_out:
                        passes = [(wh[:, k, o], xh[:, k, :]), (wh[:, k, o], xl[:, k, :]),
                                  (wl[:, k, o], xh[:, k, :])]
                    else:
                        passes = [(xh[:, k, o], wh[:, k, 0:width]), (xh[:, k, o], wl[:, k, 0:width]),
                                  (xl[:, k, o], wh[:, k, 0:width])]
                    for q, (lhs, rhs) in enumerate(passes):
                        ins = nc.tensor.matmul(bank[:, m, :], lhsT=lhs, rhs=rhs,
                                               start=(k == 0 and q == 0), stop=(k == KD - 1 and q == 2))
            ins.then_inc(slot_done.sem, 1)

        def column_part(pe, n, bank, m, parts=1, part=0):
            if m == 0 and part == 0:
                wait_slot(pe, n)
            wh = whi[:, n % RING, :].rearrange("p (k c) -> p k c", k=KD)
            wl = wlo[:, n % RING, :].rearrange("p (k c) -> p k c", k=KD)
            tok = slice(m * P, (m + 1) * P)
            for k in range(part * KD // parts, (part + 1) * KD // parts):
                for q, (lhs, w) in enumerate(((xh, wh), (xh, wl), (xl, wh))):
                    ins = nc.tensor.matmul(bank[:, m, :], lhsT=lhs[:, k, tok], rhs=w[:, k, :],
                                           start=(k == 0 and q == 0), stop=(k == KD - 1 and q == 2))
            if m == 1 and part == parts - 1:
                ins.then_inc(slot_done.sem, 1)

        def row_slot(pe, n, lh, ll, start, stop, i=0):
            wait_slot(pe, n, i)
            wh = whi[:, n % RING, :].rearrange("p (j c) -> p j c", j=2)
            wl = wlo[:, n % RING, :].rearrange("p (j c) -> p j c", j=2)
            for t in range(NT):
                tok = slice(t * P, (t + 1) * P)
                for j in range(2):
                    for q, (lhs, w) in enumerate(((lh, wh), (lh, wl), (ll, wh))):
                        for c in range(2):
                            cc = slice(c * 512, (c + 1) * 512)
                            ins = nc.tensor.matmul(Y[:, t, cc], lhsT=lhs[:, j, tok], rhs=w[:, j, cc],
                                                   start=(start and j == 0 and q == 0),
                                                   stop=(stop and j == 1 and q == 2), skip_group_check=True)
                if stop and t == 0:
                    ins.then_inc(half_done.sem, 1)
            ins.then_inc(slot_done.sem, 1)

        def inverse_root(dve, n, scale, c0=0):
            a, y, t = (m[:, c0:c0 + n] for m in (ss, rs, rt))
            v = nc.vector
            vlink(dve, v.tensor_scalar(a, a, scale, EPS, ALU.mult, ALU.add))
            vlink(dve, v.tensor_scalar(y.bitcast(I32), a.bitcast(I32), 1, None, ALU.logical_shift_right))
            vlink(dve, v.tensor_scalar(y.bitcast(I32), y.bitcast(I32), -1.0, float(0x5F3759DF),
                                       ALU.mult, ALU.add))
            for _ in range(3):
                if n == 1:
                    vlink(dve, v.scalar_tensor_tensor(t, y, a, y, ALU.mult, ALU.mult))
                else:
                    vlink(dve, v.tensor_tensor(t, y, y, ALU.mult))
                    vlink(dve, v.tensor_tensor(t, t, a, ALU.mult))
                vlink(dve, v.tensor_scalar(t, t, -0.5, 1.5, ALU.mult, ALU.add))
                vlink(dve, v.tensor_tensor(y, y, t, ALU.mult))

        def transpose_split(source, gain, hi=xh, lo=xl, k0=0, each=True):
            def g(k):
                return col[:, gain + (k0 + k if each else 0):][:, 0:1] if gain is not None else cst[:, C_ONE:C_ONE + 1]

            @block.tensor
            def _(pe):
                for t in range(NT):
                    pe.wait_ge(xn_ready.sem, xn_ready.at(t))
                    for b in range(4):
                        for kk in range(2):
                            ins = nc.tensor.transpose(A[:, b, kk * T + t * P:kk * T + (t + 1) * P],
                                                      source(t, 2 * b + kk), ident)
                        if t == NT - 1:
                            ins.then_inc(transposed.sem, 1)

            @block.scalar
            def _(act):
                for k in range(KD):
                    if k % 2 == 0:
                        act.wait_ge(transposed.sem, transposed.at(k // 2))
                    nc.scalar.activation(hi[:, k0 + k, :], A[:, k // 2, (k % 2) * T:(k % 2 + 1) * T],
                                         ACT.Identity, scale=g(k)).then_inc(xt_hi.sem, 1)

            @block.vector
            def _(dve):
                for k in range(KD):
                    if k % 2 == 0:
                        dve.wait_ge(xt_hi.sem, xt_hi.at(k + 1))
                    nc.vector.scalar_tensor_tensor(lo[:, k0 + k, :], A[:, k // 2, (k % 2) * T:(k % 2 + 1) * T],
                                                   g(k), hi[:, k0 + k, :].bitcast(F32), ALU.mult,
                                                   ALU.subtract).then_inc(xt_ready.sem, 1)

            xn_ready.passed(NT)
            transposed.passed(4)
            xt_hi.passed(KD)
            xt_ready.passed(KD)

        def pre_norm(gain):
            @block.scalar
            def _(act):
                if h_new.base == 0:
                    act.wait_ge(consts_in.sem, 16 * 3)
                for t in range(NT):
                    if h_new.base:
                        act.wait_ge(h_new.sem, h_new.base - NT + 1 + t)
                    nc.scalar.activation(xn[:, t, :], h[:, t, :], ACT.Square,
                                         accum_out=ss[:, t:t + 1]).then_inc(sq_done.sem, 1)
                act_split_upto(act, 1)

            @block.vector
            def _(dve):
                for t in range(NT):
                    dve.wait_ge(sq_done.sem, sq_done.at(t))
                    inverse_root(dve, 1, 1.0 / D, t)
                    nc.vector.tensor_scalar(xn[:, t, :], h[:, t, :], rs[:, t:t + 1], None,
                                            ALU.mult).then_inc(xn_ready.sem, 1)
                dve_split_upto(dve, 1)

            sq_done.passed(NT)
            transpose_split(lambda t, k: xn[:, t, k * P:(k + 1) * P], COLS[gain])

        def post_norm(factor):
            i = st.norms
            st.norms += 1
            row = gains[:, i % 2, :]

            @block.scalar
            def _(act):
                for t in range(NT):
                    wait_product(act, t)
                    nc.scalar.activation(xn[:, t, :], Y[:, t, :], ACT.Square,
                                         accum_out=ss[:, t:t + 1]).then_inc(sq_done.sem, 1)

            @block.vector
            def _(dve):
                dve.wait_ge(gain_in[i % 2].sem, 16 * (i // 2 + 1))
                for t in range(NT):
                    dve.wait_ge(sq_done.sem, sq_done.at(t))
                    inverse_root(dve, 1, 1.0 / D, t)
                    vlink(dve, nc.vector.scalar_tensor_tensor(xn[:, t, :], Y[:, t, :], rs[:, t:t + 1], row,
                                                              ALU.mult, ALU.mult))
                    nc.vector.scalar_tensor_tensor(h[:, t, :], xn[:, t, :], factor, h[:, t, :],
                                                   ALU.mult, ALU.add).then_inc(h_new.sem, 1)

            sq_done.passed(NT)
            h_new.passed(NT)

            if i + 2 < 6:
                @block.gpsimd
                def _(pool):
                    pool.wait_ge(h_new.sem, h_new.base)
                    pool.dma_start(gains[:, i % 2, :], rows["post"][i + 2:i + 3, :].partition_broadcast(P)
                                   .rearrange("p o d -> p (o d)")).then_inc(gain_in[i % 2].sem, 16)

        def ffn(steps, combine=None):
            n0 = st.slot
            loops = (steps - 1) // 2
            local = ExitStack()
            tag = f"_{n0}"
            gs = sb("gs" + tag, [P, 2, 2, T], where=local)
            hf = sb("hf" + tag, [P, 2, T], where=local)
            hh = sb("hh" + tag, [P, 2, 2, T], F32R, where=local)
            hl = sb("hl" + tag, [P, 2, 2, T], F32R, where=local)

            def first_slot(s):
                return n0 if s == 0 else n0 + 2 + 3 * (s - 1)

            def banks(s):
                b = 2 * (s % 2)
                return [A[:, b + j, :].rearrange("p (f t) -> p f t", f=2) for j in range(2)]

            @block.tensor
            def _(pe):
                pe.wait_ge(zero_ready.sem, 1)
                pe.wait_ge(group_free.sem, 1)
                for t in range(NT):
                    for c in range(2):
                        nc.tensor.matmul(Y[:, t, c * 512:(c + 1) * 512], lhsT=zero[:, 0:P], rhs=zero[:, :],
                                         start=True, stop=False, skip_group_check=True)
                for j in range(2):
                    column_slot(pe, n0 + j, banks(0)[j], True, first=(j == 0))

                def step(s, i=0):
                    n = first_slot(s)
                    pe.wait_ge(group_free.sem, group_free.at(s - 2) + 2 * i)
                    for j in range(2):
                        column_slot(pe, n + j, banks(s)[j], True, i=i)
                    pe.wait_ge(h_ready.sem, h_ready.at(s - 1) + 2 * i)
                    row_slot(pe, n + 2, hh[:, (s - 1) % 2], hl[:, (s - 1) % 2], False, False, i)

                with pe.Fori(0, loops) as i:
                    for s in (1, 2):
                        step(s, i)
                for s in range(1 + 2 * loops, steps):
                    step(s)
                pe.wait_ge(h_ready.sem, h_ready.at(steps - 1))
                row_slot(pe, n0 + 3 * steps - 1, hh[:, (steps - 1) % 2], hl[:, (steps - 1) % 2], False, True)
                half_done.passed(1)

            @block.scalar
            def _(act):
                def silu(s, i=0):
                    act.wait_ge(slot_done.sem, first_slot(s) + 1 + 6 * i)
                    if s:
                        act.wait_ge(group_free.sem, group_free.at(s - 2) + 2 * i)
                    nc.scalar.activation(gs[:, s % 2], banks(s)[0], ACT.Silu).then_inc(silu_ready.sem, 1)

                act_split_upto(act, n0 + 2)
                silu(0)
                act_split_upto(act, n0 + 4)
                with act.Fori(0, loops) as i:
                    for s in (1, 2):
                        silu(s, i)
                        for m in (3, 4, 5):
                            split_hi(act, first_slot(s) + m, i)
                st.act_split += 6 * loops
                for s in range(1 + 2 * loops, steps):
                    silu(s)
                    act_split_upto(act, first_slot(s) + 5)

            @block.vector
            def _(dve):
                def inner(s, i=0, e=0):
                    dve.wait_ge(silu_ready.sem, silu_ready.at(s) + 2 * i)
                    if combine is not None:
                        c = combine[:, bass.ds(e, 1), :].broadcast_to([P, 2, T])
                        vlink(dve, nc.vector.tensor_tensor(gs[:, s % 2], gs[:, s % 2], c, ALU.mult))
                    dve.wait_ge(slot_done.sem, first_slot(s) + 2 + 6 * i)
                    if s:
                        dve.wait_ge(h_ready.sem, h_ready.at(s - 1) + 2 * i)
                    nc.vector.tensor_tensor(hf[:, :, :], gs[:, s % 2], banks(s)[1],
                                            ALU.mult).then_inc(group_free.sem, 1)
                    dve.wait_ge(group_free.sem, group_free.at(s) + 2 * i)
                    vlink(dve, nc.vector.tensor_copy(hh[:, s % 2], hf[:, :, :]))
                    nc.vector.tensor_tensor(hl[:, s % 2], hf[:, :, :], hh[:, s % 2].bitcast(F32),
                                            ALU.subtract).then_inc(h_ready.sem, 1)

                dve_split_upto(dve, n0 + 3)
                inner(0)
                dve_split_upto(dve, n0 + 4)
                before = vlink.count
                with dve.Fori(0, loops) as i:
                    per = 4 if combine is not None else 2
                    vlink.loop = per * i
                    for s in (1, 2):
                        n = first_slot(s)
                        split_lo(dve, n + 3, i)
                        inner(s, i, 2 * i + s)
                        split_lo(dve, n + 4, i)
                        split_lo(dve, n + 5, i)
                assert vlink.count - before == per
                vlink.loop = 0
                vlink.count = before + per * loops
                st.dve_split += 6 * loops
                for s in range(1 + 2 * loops, steps):
                    n = first_slot(s)
                    dve_split_upto(dve, n + 3)
                    inner(s, e=s)
                    dve_split_upto(dve, n + 5)

            group_free.passed(steps)
            silu_ready.passed(steps)
            h_ready.passed(steps)
            st.slot = n0 + 3 * steps
            local.close()

        def gated_conv():
            n0 = st.slot
            local = ExitStack()
            cg = sb("cg", [P, 2, T], where=local)
            u = sb("u", [P, 2, T + 2], where=local)
            yc = sb("yc", [P, 2, T], where=local)
            hh = sb("hh_conv", [P, 2, 2, T], F32R, where=local)
            hl = sb("hl_conv", [P, 2, 2, T], F32R, where=local)
            steps = D // 256

            def first_slot(j):
                return n0 if j == 0 else n0 + 3 + 4 * (j - 1)

            def bank(kind, j):
                return A[:, [3 * (j % 2), 1, 2][kind], :].rearrange("p (f t) -> p f t", f=2)

            @block.tensor
            def _(pe):
                for j in range(steps):
                    n = first_slot(j)
                    if j >= 2:
                        pe.wait_ge(group_free.sem, group_free.at(j - 2))
                    column_slot(pe, n, bank(0, j), True, first=(j == 0))
                    if j:
                        pe.wait_ge(c_copied.sem, c_copied.at(j - 1))
                    column_slot(pe, n + 1, bank(1, j), True)
                    if j:
                        pe.wait_ge(u_ready.sem, u_ready.at(j - 1))
                    column_slot(pe, n + 2, bank(2, j), True)
                    if j:
                        pe.wait_ge(h_ready.sem, h_ready.at(j - 1))
                        row_slot(pe, n + 3, hh[:, (j - 1) % 2], hl[:, (j - 1) % 2], j == 1, False)
                pe.wait_ge(h_ready.sem, h_ready.at(steps - 1))
                row_slot(pe, n0 + 15, hh[:, (steps - 1) % 2], hl[:, (steps - 1) % 2], False, True)
                half_done.passed(1)

            @block.scalar
            def _(act):
                for j in range(steps):
                    n = first_slot(j)
                    act_split_upto(act, n + 3)
                    act.wait_ge(slot_done.sem, n + 2)
                    if j:
                        act.wait_ge(u_ready.sem, u_ready.at(j - 1))
                    nc.scalar.activation(cg[:, :, :], bank(1, j), ACT.Copy).then_inc(c_copied.sem, 1)
                    act_split_upto(act, n + 4)

            @block.vector
            def _(dve):
                v = nc.vector
                vlink(dve, v.memset(u[:, :, 0:2], 0.0))
                for j in range(steps):
                    n = first_slot(j)
                    dve_split_upto(dve, n + 4)
                    dve.wait_ge(slot_done.sem, n + 3)
                    dve.wait_ge(c_copied.sem, c_copied.at(j))
                    if j:
                        dve.wait_ge(h_ready.sem, h_ready.at(j - 1))
                    v.tensor_tensor(u[:, :, 2:], cg[:, :, :], bank(2, j), ALU.mult).then_inc(u_ready.sem, 1)
                    dve.wait_ge(u_ready.sem, u_ready.at(j))
                    for f in range(2):
                        def tap(w):
                            c = COLS["conv_k"] + 8 * w + 2 * j + f
                            return col[:, c:c + 1]
                        vlink(dve, v.tensor_scalar(yc[:, f, :], u[:, f, 2:], tap(2), None, ALU.mult))
                        for w in (1, 0):
                            vlink(dve, v.scalar_tensor_tensor(yc[:, f, :], u[:, f, w:w + T], tap(w), yc[:, f, :],
                                                              ALU.mult, ALU.add))
                    v.tensor_tensor(yc[:, :, :], yc[:, :, :], bank(0, j), ALU.mult).then_inc(group_free.sem, 1)
                    dve.wait_ge(group_free.sem, group_free.at(j))
                    vlink(dve, v.tensor_copy(hh[:, j % 2], yc[:, :, :]))
                    v.tensor_tensor(hl[:, j % 2], yc[:, :, :], hh[:, j % 2].bitcast(F32),
                                    ALU.subtract).then_inc(h_ready.sem, 1)

            for s in (group_free, c_copied, u_ready, h_ready):
                s.passed(steps)
            st.slot = n0 + 16
            finish_splits()
            local.close()

        def finish_splits():
            @block.scalar
            def _(act):
                act_split_upto(act, st.slot + 1)

            @block.vector
            def _(dve):
                dve_split_upto(dve, st.slot + 1)

        def project(count, features_out, evacuate, width=256, nbanks=4):
            n0 = st.slot
            earlier = act_free.base

            @block.tensor
            def _(pe):
                if earlier:
                    pe.wait_ge(act_free.sem, earlier)
                for j in range(count):
                    if j >= nbanks:
                        pe.wait_ge(act_free.sem, act_free.at(j - nbanks))
                    w = width if j == count - 1 else 256
                    bank = A[:, j % nbanks, 0:2 * w].rearrange("p (m c) -> p m c", m=2)
                    column_slot(pe, n0 + j, bank, features_out, w, first=(j == 0))

            @block.scalar
            def _(act):
                for j in range(count):
                    act_split_upto(act, n0 + j + 2)
                    act.wait_ge(slot_done.sem, n0 + j + 1)
                    w = width if j == count - 1 else 256
                    bank = A[:, j % nbanks, 0:2 * w].rearrange("p (m c) -> p m c", m=2)
                    evacuate(j, bank).then_inc(act_free.sem, 1)

            st.slot = n0 + count

            @block.vector
            def _(dve):
                dve_split_upto(dve, st.slot + 1)

            @block.scalar
            def _(act):
                act_split_upto(act, st.slot + 1)

            act_free.passed(count)

        def rows_product(count, lh, ll, y_used=None):
            n0 = st.slot
            ready = xt_ready.base

            @block.tensor
            def _(pe):
                pe.wait_ge(xt_ready.sem, ready)
                if y_used is not None:
                    pe.wait_ge(*y_used)
                for j in range(count):
                    row_slot(pe, n0 + j, lh[:, 2 * j:2 * j + 2], ll[:, 2 * j:2 * j + 2], j == 0, j == count - 1)
                half_done.passed(1)

            st.slot = n0 + count
            finish_splits()

        def key_value(kt, vt):
            project(4, True, lambda j, bank: nc.scalar.activation(kt[:, 2 * j:2 * j + 2, :], bank, ACT.Copy))
            rows_product(4, xh, xl)

            @block.scalar
            def _(act):
                for t in range(NT):
                    wait_product(act, t)
                    nc.scalar.activation(vt[:, t, :], Y[:, t, :], ACT.Copy).then_inc(side.sem, 1)
            side.passed(NT)

        def diff_attention(kt, vt):
            local = ExitStack()
            qt = sb("qt", [P, KD, T], where=local)
            ac = sb("ac", [P, 2, NT, T], where=local)
            lam = sb("lam_sb", [P, 4, HD], where=local)
            lm = sb("lm", [P, 8], where=local)
            bb = sb("bb", [P, T], where=local)
            sm = sb("sm", [P, 2, 2, T], where=local)
            ex = sb("ex", [P, 2, 2, T], where=local)
            aa = sb("aa", [P, 2, T], where=local)
            at = sb("at", [P, 2, T], where=local)
            nm = sb("nm", [P, 2, 2], where=local)
            su = sb("su", [P, 2, 2], where=local)
            rc = sb("rc", [P, 2], where=local)
            units = [(hd, qb) for hd in range(HEADS1) for qb in range(NT)]
            scale = HD ** -0.5
            start = h_new.base

            @block.gpsimd
            def _(pool):
                pool.wait_ge(h_new.sem, start)
                pool.dma_start(ac[:, :, :, :], attn_const.rearrange("p (a t k) -> p a t k", a=2, t=NT)
                               ).then_inc(phase_in[0].sem, 16)
                pool.dma_start(lam[:, :, :], lam_in.partition_broadcast(P)).then_inc(phase_in[0].sem, 16)

            project(4, True, lambda j, bank: nc.scalar.activation(qt[:, 2 * j:2 * j + 2, :], bank, ACT.Copy))
            q_copied = act_free.base

            @block.vector
            def _(dve):
                v = nc.vector
                dve.wait_ge(phase_in[0].sem, 32)
                vlink(dve, v.tensor_tensor(lam[:, 0::2, :], lam[:, 0::2, :], lam[:, 1::2, :], ALU.mult))
                v.tensor_reduce(lm[:, 0:2], lam[:, 0::2, :], X, ALU.add).then_inc(ask.sem, 1)
                dve.wait_ge(side.sem, side.at(0))
                vlink(dve, v.tensor_tensor(lm[:, 4:5], lm[:, 3:4], lm[:, 2:3], ALU.subtract))
                vlink(dve, v.tensor_scalar(lm[:, 5:6], lm[:, 4:5], -LAMBDA_INIT, None, ALU.add))

            @block.scalar
            def _(act):
                act.wait_ge(ask.sem, ask.at(0))
                nc.scalar.activation(lm[:, 2:4], lm[:, 0:2], ACT.Exp).then_inc(side.sem, 1)
            ask.passed(1)
            side.passed(1)

            @block.tensor
            def _(pe):
                pe.wait_ge(act_free.sem, q_copied)
                pe.wait_ge(side.sem, side.base)

                def scores(n):
                    hd, qb = units[n]
                    nk = (qb + 1) * P
                    if n:
                        pe.wait_ge(m_ready.sem, m_ready.at(n - 1))
                    for c in range(2):
                        f = slice(c * HD, (c + 1) * HD)
                        ins = nc.tensor.matmul(A[:, c, 0:nk], lhsT=qt[f, hd, qb * P:(qb + 1) * P],
                                               rhs=kt[f, hd, 0:nk], start=True, stop=True)
                    ins.then_inc(s_ready.sem, 1)

                def turn(n):
                    hd, qb = units[n]
                    pe.wait_ge(a_ready.sem, a_ready.at(n))
                    for kb in range(qb + 1):
                        ins = nc.tensor.transpose(A[:, 2 + n % 2, kb * P:(kb + 1) * P],
                                                  aa[:, n % 2, kb * P:(kb + 1) * P], ident)
                    ins.then_inc(at_ready.sem, 1)

                def output(n):
                    hd, qb = units[n]
                    pe.wait_ge(at_copied.sem, at_copied.at(n))
                    for kb in range(qb + 1):
                        ins = nc.tensor.matmul(Y[:, qb, hd * P:(hd + 1) * P], lhsT=at[:, n % 2, kb * P:(kb + 1) * P],
                                               rhs=vt[:, kb, hd * P:(hd + 1) * P], start=(kb == 0), stop=(kb == qb))
                    ins.then_inc(o_ready.sem, 1)

                scores(0)
                scores(1)
                for n in range(len(units)):
                    if n + 2 < len(units):
                        scores(n + 2)
                    turn(n)
                    if n:
                        output(n - 1)
                output(len(units) - 1)

            @block.vector
            def _(dve):
                v = nc.vector

                def front(n):
                    hd, qb = units[n]
                    nk = (qb + 1) * P
                    slope = 2.0 ** (-8.0 * (hd + 1) / HEADS1)
                    vlink(dve, v.scalar_tensor_tensor(bb[:, 0:nk], ac[:, 0, qb, 0:nk], slope, ac[:, 1, qb, 0:nk],
                                                      ALU.mult, ALU.add))
                    dve.wait_ge(s_ready.sem, s_ready.at(n))
                    vlink(dve, v.scalar_tensor_tensor(
                        sm[:, n % 2, :, 0:nk], A[:, 0:2, 0:nk], scale,
                        bb[:, 0:nk].unsqueeze(1).broadcast_to([P, 2, nk]), ALU.mult, ALU.add))
                    v.tensor_reduce(nm[:, n % 2, :], sm[:, n % 2, :, 0:nk], X, ALU.max,
                                    negate=True).then_inc(m_ready.sem, 1)

                def back(n):
                    nk = (units[n][1] + 1) * P
                    dve.wait_ge(e_ready.sem, e_ready.at(n))
                    if n:
                        dve.wait_ge(a_ready.sem, a_ready.at(n - 1))
                    vlink(dve, v.reciprocal(rc[:, :], su[:, n % 2, :]))
                    vlink(dve, v.tensor_tensor(rc[:, 1:2], rc[:, 1:2], lm[:, 5:6], ALU.mult))
                    if n >= 2:
                        dve.wait_ge(at_ready.sem, at_ready.at(n - 2))
                    vlink(dve, v.tensor_scalar(aa[:, n % 2, 0:nk], ex[:, n % 2, 0, 0:nk], rc[:, 0:1], None, ALU.mult))
                    v.scalar_tensor_tensor(aa[:, n % 2, 0:nk], ex[:, n % 2, 1, 0:nk], rc[:, 1:2],
                                           aa[:, n % 2, 0:nk], ALU.mult, ALU.add).then_inc(a_ready.sem, 1)

                front(0)
                for n in range(len(units)):
                    if n + 1 < len(units):
                        front(n + 1)
                    back(n)

            @block.scalar
            def _(act):
                def copy(n):
                    nk = (units[n][1] + 1) * P
                    act.wait_ge(at_ready.sem, at_ready.at(n))
                    if n >= 2:
                        act.wait_ge(o_ready.sem, o_ready.at(n - 2))
                    nc.scalar.activation(at[:, n % 2, 0:nk], A[:, 2 + n % 2, 0:nk],
                                         ACT.Copy).then_inc(at_copied.sem, 1)

                for n in range(len(units)):
                    nk = (units[n][1] + 1) * P
                    act.wait_ge(m_ready.sem, m_ready.at(n))
                    if n >= 2:
                        act.wait_ge(a_ready.sem, a_ready.at(n - 2))
                    for c in range(2):
                        ins = nc.scalar.activation(ex[:, n % 2, c, 0:nk], sm[:, n % 2, c, 0:nk], ACT.Exp,
                                                   bias=nm[:, n % 2, c:c + 1], accum_out=su[:, n % 2, c:c + 1])
                    ins.then_inc(e_ready.sem, 1)
                    if n:
                        copy(n - 1)
                copy(len(units) - 1)
                act.wait_ge(o_ready.sem, o_ready.at(len(units) - 1))
                for t in range(NT):
                    nc.scalar.activation(xn[:, t, :], Y[:, t, :], ACT.Square).then_inc(sq_done.sem, 1)

            @block.vector
            def _(dve):
                v = nc.vector
                for t in range(NT):
                    dve.wait_ge(sq_done.sem, sq_done.at(t))
                    vlink(dve, v.tensor_reduce(ss[:, t * HEADS1:(t + 1) * HEADS1],
                                               xn[:, t, :].rearrange("p (h e) -> p h e", h=HEADS1), X, ALU.add))
                inverse_root(dve, NT * HEADS1, 1.0 / P)
                vlink(dve, v.tensor_scalar(rs[:, 0:16], rs[:, 0:16], 1.0 - LAMBDA_INIT, None, ALU.mult))
                for t in range(NT):
                    r = rs[:, t * HEADS1:(t + 1) * HEADS1].unsqueeze(2).broadcast_to([P, HEADS1, P])
                    v.tensor_tensor(xn[:, t, :].rearrange("p (h e) -> p h e", h=HEADS1),
                                    Y[:, t, :].rearrange("p (h e) -> p h e", h=HEADS1), r,
                                    ALU.mult).then_inc(xn_ready.sem, 1)

            for s in (s_ready, m_ready, e_ready, a_ready, at_ready, at_copied, o_ready):
                s.passed(len(units))
            sq_done.passed(NT)
            transpose_split(lambda t, k: xn[:, t, k * P:(k + 1) * P], COLS["subln"], each=False)
            finish_splits()
            rows_product(4, xh, xl)
            local.close()

        def sparse_attention(ya_hi, ya_lo, iw, zs):
            local = ExitStack()
            tok = sb("tok", [P, NT, ROPED * HD], where=local)
            vv = sb("vv", [P, NT, T], where=local)
            k2 = sb("k2", [P, NT, 5, 2, HD], where=local)
            qt = sb("qt2", [P, 18, T], where=local)
            gr = sb("gr", [P, 3, HD], where=local)
            adm = sb("adm", [P, NT, T], where=local)
            score = sb("score", [P, NT, T], where=local)
            m8 = sb("m8", [P, 8], where=local)
            sm = sb("sm2", [P, 2, 2, T], where=local)
            ex = sb("ex2", [P, 2, 2, T], where=local)
            at = sb("at2", [P, 2, 512], where=local)
            nm = sb("nm2", [P, 2, 2], where=local)
            su = sb("su2", [P, 2, 2], where=local)
            rc = sb("rc2", [P, 2], where=local)
            flat = xn[:, :, :].rearrange("p t d -> p (t d)")
            start = h_new.base

            @block.gpsimd
            def _(pool):
                pool.wait_ge(h_new.sem, start)
                pool.dma_start(adm[:, :, :], adm_const.rearrange("p (t k) -> p t k", t=NT)
                               ).then_inc(phase_in[1].sem, 16)
                pool.dma_start(gr[:, :, :], rows["qk"].partition_broadcast(P)).then_inc(phase_in[1].sem, 16)

            def evacuate(j, bank):
                if j < 5:
                    return nc.scalar.activation(tok[:, :, j * 256:(j + 1) * 256], bank, ACT.Copy)
                if j < 7:
                    at_ = NORMED * HD + (j - 5) * 256
                    return nc.scalar.activation(tok[:, :, at_:at_ + 256], bank, ACT.Copy)
                if j == 7:
                    return nc.scalar.activation(vv[:, :, :], bank, ACT.Copy)
                nc.scalar.activation(tok[:, :, 1280:1344], bank[:, :, 0:64], ACT.Copy)
                nc.scalar.activation(iw[:, :, :], bank[:, :, 64:72], ACT.Copy)
                return nc.scalar.activation(dt_raw[:, :, :], bank[:, :, 72:104], ACT.Copy)

            project(9, False, evacuate, width=104)
            ready = act_free.base
            z0 = st.slot
            z_early = 4

            def bank_of_z(b):
                return A[:, b, :].rearrange("p (m c) -> p m c", m=2)

            def copy_z(act, j, b):
                act.wait_ge(slot_done.sem, z0 + j + 1)
                nc.scalar.activation(zs[:, :, j * 256:(j + 1) * 256], bank_of_z(b),
                                     ACT.Copy).then_inc(act_free.sem, 1)

            @block.tensor
            def _(pe):
                pe.wait_ge(act_free.sem, ready)
                for j in range(z_early):
                    for m in range(2):
                        column_part(pe, z0 + j, bank_of_z(j), m)

            @block.scalar
            def _(act):
                act.wait_ge(act_free.sem, ready)
                for t in range(NT):
                    if t:
                        act.wait_ge(ask.sem, ask.at(t - 1))
                    nc.scalar.activation(flat[:, 0:NORMED * HD], tok[:, t, 0:NORMED * HD],
                                         ACT.Square).then_inc(sq_done.sem, 1)
                for j in range(z_early):
                    act_split_upto(act, z0 + j + 2)
                    copy_z(act, j, j)

            @block.vector
            def _(dve):
                v = nc.vector
                dve.wait_ge(phase_in[1].sem, 32)
                dve.wait_ge(act_free.sem, ready)
                for t in range(NT):
                    dve.wait_ge(sq_done.sem, sq_done.at(t))
                    v.tensor_reduce(ss[:, t * NORMED:(t + 1) * NORMED],
                                    flat[:, 0:NORMED * HD].rearrange("p (h e) -> p h e", e=HD), X,
                                    ALU.add).then_inc(ask.sem, 1)
                    dve.wait_ge(ask.sem, ask.at(t))
                inverse_root(dve, NT * NORMED, 1.0 / HD)
                dve_split_upto(dve, z0 + 2)
                vlink(dve, v.tensor_scalar(iw[:, :, :], iw[:, :, :], IDX_HEADS ** -0.5, None, ALU.mult))
                tmp = flat[:, 0:4 * ROPED * 8].rearrange("p (a h e) -> p a h e", a=4, e=8)
                for t in range(NT):
                    hv = tok[:, t, :].rearrange("p (h e) -> p h e", e=HD)
                    r = rs[:, t * NORMED:(t + 1) * NORMED].unsqueeze(2).broadcast_to([P, NORMED, HD])
                    vlink(dve, v.tensor_tensor(hv[:, 0:NORMED, :], hv[:, 0:NORMED, :], r, ALU.mult))
                    for i, (a, b) in enumerate(((0, 16), (16, 20), (20, 21))):
                        g = gr[:, i:i + 1, :].broadcast_to([P, b - a, HD])
                        ins = v.tensor_tensor(hv[:, a:b, :], hv[:, a:b, :], g, ALU.mult)
                    vlink(dve, ins)
                    c = cst[:, C_COS + 8 * t:C_COS + 8 * t + 8].unsqueeze(1).broadcast_to([P, ROPED, 8])
                    s = cst[:, C_SIN + 8 * t:C_SIN + 8 * t + 8].unsqueeze(1).broadcast_to([P, ROPED, 8])
                    x1, x2 = hv[:, :, 0:8], hv[:, :, 8:16]
                    for i, (a, b) in enumerate(((x1, c), (x2, s), (x2, c), (x1, s))):
                        ins = v.tensor_tensor(tmp[:, i], a, b, ALU.mult)
                    vlink(dve, ins)
                    v.tensor_tensor(x1, tmp[:, 0], tmp[:, 1], ALU.subtract)
                    vlink(dve, v.tensor_tensor(x2, tmp[:, 2], tmp[:, 3], ALU.add))
                    v.tensor_copy(k2[:, t, :, :, :], hv[:, 16:21, :].unsqueeze(2).broadcast_to([P, 5, 2, HD])
                                  ).then_inc(xn_ready.sem, 1)
                    dve.wait_ge(xn_ready.sem, xn_ready.at(t))
                    dve_split_upto(dve, z0 + 3 + 2 * t)

            act_free.passed(z_early)
            z_copied = act_free.base

            def tile_of(m, t):
                if m < 8:
                    return tok[:, t, m * P:(m + 1) * P]
                if m < 12:
                    return tok[:, t, NORMED * HD + (m - 8) * P:NORMED * HD + (m - 7) * P]
                return k2[:, t, m - 12, :, :].rearrange("p a e -> p (a e)")

            @block.tensor
            def _(pe):
                pe.wait_ge(act_free.sem, z_copied)
                for t in range(NT):
                    pe.wait_ge(xn_ready.sem, xn_ready.at(t))
                for m in range(17):
                    if m % 2 == 0 and m >= 8:
                        pe.wait_ge(act_free.sem, act_free.at(m // 2 - 4))
                    for t in range(NT):
                        at_ = (m % 2) * T + t * P
                        ins = nc.tensor.transpose(A[:, (m // 2) % 4, at_:at_ + P], tile_of(m, t), ident)
                    if m % 2 or m == 16:
                        ins.then_inc(transposed.sem, 1)

            @block.scalar
            def _(act):
                for g in range(9):
                    act.wait_ge(transposed.sem, transposed.at(g))
                    w = 512 if g < 8 else 256
                    nc.scalar.activation(qt[:, 2 * g:2 * g + w // T, :],
                                         A[:, g % 4, 0:w].rearrange("p (m t) -> p m t", t=T),
                                         ACT.Copy).then_inc(act_free.sem, 1)
            xn_ready.passed(NT)
            transposed.passed(9)
            act_free.passed(9)
            sq_done.passed(NT)
            ask.passed(NT)
            turned = act_free.base

            idx_units = [(t, p) for t in range(NT) for p in range(IDX_HEADS // 2)]

            @block.tensor
            def _(pe):
                pe.wait_ge(act_free.sem, turned)
                for n, (t, p) in enumerate(idx_units):
                    nk = (t + 1) * P
                    if n >= 2:
                        pe.wait_ge(e_ready.sem, e_ready.at(n - 2))
                    for c in range(2):
                        f = slice(c * HD, (c + 1) * HD)
                        ins = nc.tensor.matmul(A[:, 2 * (n % 2) + c, 0:nk], lhsT=qt[f, 8 + p, t * P:(t + 1) * P],
                                               rhs=qt[f, 16, 0:nk], start=True, stop=True)
                    ins.then_inc(s_ready.sem, 1)

            @block.scalar
            def _(act):
                for n, (t, p) in enumerate(idx_units):
                    nk = (t + 1) * P
                    act.wait_ge(s_ready.sem, s_ready.at(n))
                    if n >= 2:
                        act.wait_ge(a_ready.sem, a_ready.at(n - 2))
                    b = 2 * (n % 2)
                    nc.scalar.activation(ex[:, n % 2, :, 0:nk], A[:, b:b + 2, 0:nk], ACT.Relu,
                                         scale=HD ** -0.5).then_inc(e_ready.sem, 1)

            @block.vector
            def _(dve):
                v = nc.vector
                for n, (t, p) in enumerate(idx_units):
                    nk = (t + 1) * P
                    dve.wait_ge(e_ready.sem, e_ready.at(n))
                    sc = score[:, t, 0:nk]
                    for c in range(2):
                        w = iw[:, t, 2 * p + c:2 * p + c + 1]
                        if p == 0 and c == 0:
                            vlink(dve, v.tensor_scalar(sc, ex[:, n % 2, 0, 0:nk], w, None, ALU.mult))
                        elif c == 0:
                            vlink(dve, v.scalar_tensor_tensor(sc, ex[:, n % 2, 0, 0:nk], w, sc, ALU.mult, ALU.add))
                        else:
                            v.scalar_tensor_tensor(sc, ex[:, n % 2, 1, 0:nk], w, sc, ALU.mult,
                                                   ALU.add).then_inc(a_ready.sem, 1)
                            dve.wait_ge(a_ready.sem, a_ready.at(n))
                    if p == IDX_HEADS // 2 - 1:
                        vlink(dve, v.tensor_tensor(sc, sc, adm[:, t, 0:nk], ALU.add))
                        for _ in range(TOPK // 8):
                            vlink(dve, v.max(m8[:, :], sc))
                            vlink(dve, v.match_replace(sc, m8[:, :], sc, TAKEN))
                        vlink(dve, v.tensor_scalar(sc, sc, TAKEN * 0.9, NEG, ALU.is_gt, ALU.mult))

            for s in (s_ready, e_ready, a_ready):
                s.passed(len(idx_units))

            units = [(t, p) for t in range(NT) for p in range(HEADS2 // 2)]
            z1 = z0 + z_early
            z_late = 4

            @block.tensor
            def _(pe):
                pe.wait_ge(e_ready.sem, e_ready.base)

                def scores(n):
                    t, p = units[n]
                    nk = (t + 1) * P
                    if n:
                        pe.wait_ge(m_ready.sem, m_ready.at(n - 1))
                    for c in range(2):
                        f = slice(c * HD, (c + 1) * HD)
                        ins = nc.tensor.matmul(A[:, c, 0:nk], lhsT=qt[f, p, t * P:(t + 1) * P],
                                               rhs=qt[f, 12 + p // 2, 0:nk], start=True, stop=True)
                    ins.then_inc(s_ready.sem, 1)

                def turn(n):
                    t, p = units[n]
                    pe.wait_ge(a_ready.sem, a_ready.at(n))
                    for c in range(2):
                        for kb in range(t + 1):
                            at_ = (c * (t + 1) + kb) * P
                            ins = nc.tensor.transpose(A[:, 2, at_:at_ + P],
                                                      ex[:, n % 2, c, kb * P:(kb + 1) * P], ident)
                    ins.then_inc(at_ready.sem, 1)

                def output(n):
                    t, p = units[n]
                    pe.wait_ge(at_copied.sem, at_copied.at(n))
                    kv = p // 2
                    for c in range(2):
                        for kb in range(t + 1):
                            at_ = (c * (t + 1) + kb) * P
                            ins = nc.tensor.matmul(YT[c * HD:(c + 1) * HD, p, t * P:(t + 1) * P],
                                                   lhsT=vv[:, kb, kv * HD:(kv + 1) * HD],
                                                   rhs=at[:, n % 2, at_:at_ + P], start=(kb == 0), stop=(kb == t))
                    ins.then_inc(o_ready.sem, 1)

                scores(0)
                for n in range(len(units)):
                    if n + 1 < len(units):
                        scores(n + 1)
                    if n and n % 4 == 0:
                        pe.wait_ge(act_free.sem, act_free.at(n // 4 - 1))
                    column_part(pe, z1 + n // 4, bank_of_z(3), n // 2 % 2, 2, n % 2)
                    if n:
                        output(n - 1)
                    turn(n)
                output(len(units) - 1)

            @block.vector
            def _(dve):
                v = nc.vector

                def front(n):
                    t, p = units[n]
                    nk = (t + 1) * P
                    dve.wait_ge(s_ready.sem, s_ready.at(n))
                    vlink(dve, v.scalar_tensor_tensor(
                        sm[:, n % 2, :, 0:nk], A[:, 0:2, 0:nk], HD ** -0.5,
                        score[:, t:t + 1, 0:nk].broadcast_to([P, 2, nk]), ALU.mult, ALU.add))
                    v.tensor_reduce(nm[:, n % 2, :], sm[:, n % 2, :, 0:nk], X, ALU.max,
                                    negate=True).then_inc(m_ready.sem, 1)

                def back(n):
                    nk = (units[n][0] + 1) * P
                    dve.wait_ge(e_ready.sem, e_ready.at(n))
                    if n:
                        dve.wait_ge(a_ready.sem, a_ready.at(n - 1))
                    vlink(dve, v.reciprocal(rc[:, :], su[:, n % 2, :]))
                    v.tensor_tensor(ex[:, n % 2, :, 0:nk], ex[:, n % 2, :, 0:nk],
                                    rc[:, :].unsqueeze(2).broadcast_to([P, 2, nk]),
                                    ALU.mult).then_inc(a_ready.sem, 1)

                front(0)
                for n in range(len(units)):
                    if n + 1 < len(units):
                        front(n + 1)
                    back(n)
                    if n % 4 == 0:
                        dve_split_upto(dve, z1 + n // 4 + 2)

            @block.scalar
            def _(act):
                def copy(n):
                    nk = (units[n][0] + 1) * P
                    act.wait_ge(at_ready.sem, at_ready.at(n))
                    if n >= 2:
                        act.wait_ge(o_ready.sem, o_ready.at(n - 2))
                    nc.scalar.activation(at[:, n % 2, 0:2 * nk], A[:, 2, 0:2 * nk],
                                         ACT.Copy).then_inc(at_copied.sem, 1)

                for n in range(len(units)):
                    nk = (units[n][0] + 1) * P
                    if n and n % 4 == 0:
                        copy_z(act, z_early + n // 4 - 1, 3)
                    act.wait_ge(m_ready.sem, m_ready.at(n))
                    if n >= 2:
                        act.wait_ge(at_ready.sem, at_ready.at(n - 2))
                    for c in range(2):
                        ins = nc.scalar.activation(ex[:, n % 2, c, 0:nk], sm[:, n % 2, c, 0:nk], ACT.Exp,
                                                   bias=nm[:, n % 2, c:c + 1], accum_out=su[:, n % 2, c:c + 1])
                    ins.then_inc(e_ready.sem, 1)
                    if n:
                        copy(n - 1)
                    if n % 4 == 0:
                        act_split_upto(act, z1 + n // 4 + 2)
                copy_z(act, z_early + z_late - 1, 3)
                copy(len(units) - 1)
                act.wait_ge(o_ready.sem, o_ready.at(len(units) - 1))
                for k in range(4):
                    nc.scalar.activation(ya_hi[:, 2 * k:2 * k + 2, :], YT[:, 2 * k:2 * k + 2, :],
                                         ACT.Copy).then_inc(xt_hi.sem, 1)
                act.wait_ge(act_free.sem, act_free.at(z_late - 1))
                nc.scalar.activation(zs[:, :, :], zs[:, :, :], ACT.Silu).then_inc(act_free.sem, 1)

            @block.vector
            def _(dve):
                for k in range(4):
                    dve.wait_ge(xt_hi.sem, xt_hi.at(k))
                    nc.vector.tensor_tensor(ya_lo[:, 2 * k:2 * k + 2, :], YT[:, 2 * k:2 * k + 2, :],
                                            ya_hi[:, 2 * k:2 * k + 2, :].bitcast(F32),
                                            ALU.subtract).then_inc(xt_ready.sem, 1)

            st.slot = z1 + z_late
            act_free.passed(z_late + 1)
            xt_hi.passed(4)
            xt_ready.passed(4)
            for s in (s_ready, m_ready, e_ready, a_ready, at_ready, at_copied, o_ready):
                s.passed(len(units))
            local.close()

        def state_space_inputs(xs, bt, ct):
            n0 = st.slot
            local = ExitStack()
            u = sb("u2", [P, 2, T + 3], where=local)
            yc = sb("yc2", [P, 2, 2, T], where=local)
            xt = xn[:, :, :].rearrange("p t (a b) -> p (t a) b", b=T)

            @block.tensor
            def _(pe):
                def turn(j):
                    pe.wait_ge(silu_ready.sem, silu_ready.at(j))
                    if j >= 2:
                        pe.wait_ge(act_free.sem, act_free.at(2 * j - 4 + 1))
                    for f in range(2):
                        for t in range(NT):
                            at_ = t * T + f * P
                            ins = nc.tensor.transpose(A[:, 2 + j % 2, at_:at_ + P],
                                                      xt[:, 2 * (j % 4) + f, t * P:(t + 1) * P], ident)
                    ins.then_inc(transposed.sem, 1)

                pe.wait_ge(m_ready.sem, m_ready.base)
                pe.wait_ge(act_free.sem, act_free.base - 1)
                for j in range(12):
                    if j >= 2:
                        pe.wait_ge(u_ready.sem, u_ready.at(j - 2))
                    column_slot(pe, n0 + j, A[:, j % 2, :].rearrange("p (f t) -> p f t", f=2), True)
                    if 2 <= j < 10:
                        turn(j - 2)
                pe.wait_ge(u_ready.sem, u_ready.at(11))

            @block.scalar
            def _(act):
                def copy(j):
                    act.wait_ge(transposed.sem, transposed.at(j))
                    for t in range(NT):
                        nc.scalar.activation(xs[:, t, j * 256:(j + 1) * 256], A[:, 2 + j % 2, t * T:(t + 1) * T],
                                             ACT.Copy).then_inc(act_free.sem, 1)

                def silu(j):
                    act.wait_ge(h_ready.sem, h_ready.at(j))
                    if j < 8:
                        if j >= 4:
                            act.wait_ge(transposed.sem, transposed.at(j - 4))
                        dst = xt[:, 2 * (j % 4):2 * (j % 4) + 2, :]
                    else:
                        dst = (bt if j < 10 else ct)[:, 2 * (j % 2):2 * (j % 2) + 2, :]
                    nc.scalar.activation(dst, yc[:, j % 2], ACT.Silu).then_inc(silu_ready.sem, 1)

                for j in range(12):
                    act_split_upto(act, n0 + j + 2)
                    act.wait_ge(slot_done.sem, n0 + j + 1)
                    if j:
                        act.wait_ge(h_ready.sem, h_ready.at(j - 1))
                    nc.scalar.activation(u[:, :, 3:], A[:, j % 2, :].rearrange("p (f t) -> p f t", f=2),
                                         ACT.Copy).then_inc(u_ready.sem, 1)
                    if j:
                        silu(j - 1)
                    if 3 <= j < 11:
                        copy(j - 3)
                silu(11)
                act_split_upto(act, n0 + 13)

            @block.vector
            def _(dve):
                v = nc.vector
                vlink(dve, v.memset(u[:, :, 0:3], 0.0))
                for j in range(12):
                    dve_split_upto(dve, n0 + j + 2)
                    dve.wait_ge(u_ready.sem, u_ready.at(j))
                    if j >= 2:
                        dve.wait_ge(silu_ready.sem, silu_ready.at(j - 2))
                    y = yc[:, j % 2]
                    for f in range(2):
                        m = 2 * j + f

                        def tap(w):
                            c = COLS["conv_w"] + 24 * w + m
                            return col[:, c:c + 1]
                        b = COLS["conv_b"] + m
                        vlink(dve, v.tensor_scalar(y[:, f, :], u[:, f, 3:], tap(3), col[:, b:b + 1], ALU.mult, ALU.add))
                        for w in (2, 1, 0):
                            ins = v.scalar_tensor_tensor(y[:, f, :], u[:, f, w:w + T], tap(w), y[:, f, :],
                                                         ALU.mult, ALU.add)
                            if w or f == 0:
                                vlink(dve, ins)
                    ins.then_inc(h_ready.sem, 1)
                dve_split_upto(dve, n0 + 13)

            u_ready.passed(12)
            h_ready.passed(12)
            silu_ready.passed(12)
            transposed.passed(8)
            act_free.passed(16)
            st.slot = n0 + 12
            local.close()

        def state_space(xs, zs, bt, ct, ga, gb, where):
            cb = sb("cb", [P, 4, 3 * P], where=where)
            lw = sb("lw", [P, 2, 2, P], where=where)
            ee = sb("ee", [P, 2, 3 * P], where=where)
            mm = sb("mm", [P, 2, 3 * P], where=where)
            tmp = sb("tmp", [P, 512], where=where)
            dsk = sb("dsk", [P, 3, 32], where=where)
            dd = sb("dd", [P, 8, NT * 32], where=where)
            dt = dd[:, 6].rearrange("p (t h) -> p t h", t=NT)
            da = dd[:, 7].rearrange("p (t h) -> p t h", t=NT)
            started = act_free.base
            sil = silu_ready.base

            @block.gpsimd
            def _(pool):
                pool.wait_ge(silu_ready.sem, sil)
                pool.dma_start(dsk[:, :, :], rows["ssd"].partition_broadcast(P)).then_inc(phase_in[1].sem, 16)

            @block.vector
            def _(dve):
                v = nc.vector
                dve.wait_ge(phase_in[1].sem, 48)
                x, m, e, z, z2, p = (dd[:, i] for i in range(6))
                xv = x.rearrange("p (t h) -> p t h", t=NT)
                vlink(dve, v.tensor_tensor(xv, dt_raw[:, :, :], dsk[:, 0:1, :].broadcast_to([P, NT, 32]), ALU.add))
                vlink(dve, v.tensor_scalar(m, x, -1.0, None, ALU.mult))
                vlink(dve, v.tensor_tensor(p, x, m, ALU.max))
                v.tensor_scalar(m, x, 0.0, None, ALU.max).then_inc(ask.sem, 1)
                dve.wait_ge(side.sem, side.at(1))
                vlink(dve, v.tensor_scalar(z, e, 2.0, None, ALU.add))
                vlink(dve, v.reciprocal(z, z))
                vlink(dve, v.tensor_tensor(z, z, e, ALU.mult))
                vlink(dve, v.tensor_tensor(z2, z, z, ALU.mult))
                vlink(dve, v.tensor_scalar(p, z2, 1.0 / 15, None, ALU.mult))
                for q in (13, 11, 9, 7, 5, 3):
                    vlink(dve, v.scalar_tensor_tensor(p, p, 1.0 / q, z2, ALU.add, ALU.mult))
                vlink(dve, v.scalar_tensor_tensor(p, p, 1.0, z, ALU.add, ALU.mult))
                vlink(dve, v.scalar_tensor_tensor(dd[:, 6], p, 2.0, m, ALU.mult, ALU.add))
                vlink(dve, v.scalar_tensor_tensor(da, dt, -1.0, dsk[:, 1:2, :].broadcast_to([P, NT, 32]),
                                                  ALU.mult, ALU.mult))
                for g in range(4):
                    dve.wait_ge(s_ready.sem, s_ready.at(g))
                    v.tensor_tensor(cb[:, g, :], A[:, g, 0:3 * P], cst[:, C_TRI:C_TRI + 3 * P],
                                    ALU.mult).then_inc(m_ready.sem, 1)
                dve.wait_ge(m_ready.sem, m_ready.at(3))

            @block.scalar
            def _(act):
                act.wait_ge(ask.sem, ask.at(0))
                act.wait_ge(phase_in[1].sem, 48)
                nc.scalar.activation(dd[:, 2], dd[:, 5], ACT.Exp, scale=-1.0).then_inc(side.sem, 1)
                nc.scalar.activation(dsk[:, 1, :], dsk[:, 1, :], ACT.Exp).then_inc(side.sem, 1)

            @block.tensor
            def _(pe):
                pe.wait_ge(silu_ready.sem, sil)
                pe.wait_ge(act_free.sem, started)
                for g in range(4):
                    for b, (s, l) in enumerate(((0, 0), (0, 1), (1, 1))):
                        ins = nc.tensor.matmul(A[:, g, b * P:(b + 1) * P], lhsT=bt[:, g, s * P:(s + 1) * P],
                                               rhs=ct[:, g, l * P:(l + 1) * P], start=True, stop=True)
                    ins.then_inc(s_ready.sem, 1)

            ask.passed(1)
            side.passed(2)
            s_ready.passed(4)
            m_ready.passed(4)
            masked = m_ready.base
            g0 = st.slot
            gate_bank = A[:, 3, :].rearrange("p (m c) -> p m c", m=2)

            @block.tensor
            def _(pe):
                pe.wait_ge(m_ready.sem, masked)

                def decay(n):
                    pe.wait_ge(a_ready.sem, a_ready.at(n))
                    if n >= 3:
                        pe.wait_ge(e_ready.sem, e_ready.at(n - 3))
                    tri = cst[:, C_TRI:C_TRI + P]
                    bank = A[:, n % 3, :]
                    nc.tensor.matmul(bank[:, 0:2 * P], lhsT=lw[:, n % 2, 0, :], rhs=cst[:, C_TRI:C_TRI + 2 * P],
                                     start=True, stop=False, skip_group_check=True)
                    nc.tensor.matmul(bank[:, P:2 * P], lhsT=da[:, 1, n:n + 1].broadcast_to([P, P]), rhs=tri,
                                     start=False, stop=True, skip_group_check=True)
                    nc.tensor.matmul(bank[:, 2 * P:3 * P], lhsT=lw[:, n % 2, 1, :], rhs=tri,
                                     start=True, stop=True, skip_group_check=True).then_inc(s_ready.sem, 1)

                def output(n):
                    g = n // 8
                    if n % 8 == 0 and g >= 2:
                        pe.wait_ge(group_free.sem, group_free.at(2 * (g - 2) + 1))
                    pe.wait_ge(m_ready.sem, m_ready.at(n))
                    c = slice((n % 8) * SSD_P, (n % 8 + 1) * SSD_P)
                    w = mm[:, n % 2, :]
                    x = xs[:, :, n * SSD_P:(n + 1) * SSD_P]
                    b = 2 * (g % 2)
                    nc.tensor.matmul(Y4[:, b, c], lhsT=w[:, 0:P], rhs=x[:, 0], start=True, stop=True)
                    nc.tensor.matmul(Y4[:, b + 1, c], lhsT=w[:, P:2 * P], rhs=x[:, 0], start=True, stop=False)
                    nc.tensor.matmul(Y4[:, b + 1, c], lhsT=w[:, 2 * P:3 * P], rhs=x[:, 1], start=False,
                                     stop=True).then_inc(o_ready.sem, 1)

                decay(0)
                decay(1)
                for n in range(SSD_HEADS):
                    if n + 2 < SSD_HEADS:
                        decay(n + 2)
                    if n and n % 4 == 0:
                        pe.wait_ge(act_free.sem, act_free.at(n // 4 - 1))
                    column_part(pe, g0 + n // 4, gate_bank, n // 2 % 2, 2, n % 2)
                    output(n)

            @block.scalar
            def _(act):
                def copy_gate(j):
                    act.wait_ge(slot_done.sem, g0 + j + 1)
                    nc.scalar.activation((ga if j < 4 else gb)[:, :, (j % 4) * 256:(j % 4 + 1) * 256],
                                         gate_bank, ACT.Copy).then_inc(act_free.sem, 1)

                for n in range(SSD_HEADS):
                    act.wait_ge(s_ready.sem, s_ready.at(n))
                    if n >= 2:
                        act.wait_ge(m_ready.sem, m_ready.at(n - 2))
                    nc.scalar.activation(ee[:, n % 2, :], A[:, n % 3, 0:3 * P], ACT.Exp).then_inc(e_ready.sem, 1)
                    if n % 4 == 1:
                        if n > 1:
                            copy_gate(n // 4 - 1)
                        act_split_upto(act, g0 + n // 4 + 2)
                copy_gate(7)
                act.wait_ge(act_free.sem, act_free.at(7))
                for m in (ga, gb):
                    nc.scalar.activation(m[:, :, :], m[:, :, :], ACT.Sigmoid).then_inc(act_free.sem, 1)

            @block.vector
            def _(dve):
                v = nc.vector

                def weights(n):
                    if n >= 2:
                        dve.wait_ge(s_ready.sem, s_ready.at(n - 2))
                    for t in range(NT):
                        ins = v.tensor_scalar(lw[:, n % 2, t, :], cst[:, C_GT:C_GT + P], da[:, t, n:n + 1], None,
                                              ALU.mult)
                    ins.then_inc(a_ready.sem, 1)

                def product(n):
                    dve.wait_ge(e_ready.sem, e_ready.at(n))
                    if n >= 2:
                        dve.wait_ge(o_ready.sem, o_ready.at(n - 2))
                    g = n // 8
                    v.scalar_tensor_tensor(mm[:, n % 2, 0:2 * P], ee[:, n % 2, 0:2 * P], dt[:, 0, n:n + 1],
                                           cb[:, g, 0:2 * P], ALU.mult, ALU.mult)
                    v.scalar_tensor_tensor(mm[:, n % 2, 2 * P:], ee[:, n % 2, 2 * P:], dt[:, 1, n:n + 1],
                                           cb[:, g, 2 * P:], ALU.mult, ALU.mult).then_inc(m_ready.sem, 1)

                def gate(g, tiles):
                    for t in tiles:
                        c = slice(g * 512, (g + 1) * 512)
                        sk = dsk[:, 2, 8 * g:8 * g + 8].unsqueeze(2).broadcast_to([P, 8, SSD_P])
                        vlink(dve, v.tensor_tensor(tmp[:, :].rearrange("p (h e) -> p h e", h=8),
                                                   xs[:, t, c].rearrange("p (h e) -> p h e", h=8), sk, ALU.mult))
                        if t == 0:
                            dve.wait_ge(o_ready.sem, o_ready.at(8 * g + 7))
                        v.tensor_tensor(tmp[:, :], tmp[:, :], Y4[:, 2 * (g % 2) + t, :],
                                        ALU.add).then_inc(group_free.sem, 1)
                        dve.wait_ge(group_free.sem, group_free.at(2 * g + t))
                        vlink(dve, v.tensor_tensor(zs[:, t, c], zs[:, t, c], tmp[:, :], ALU.mult))
                        i = t * 4 + g
                        vlink(dve, v.scalar_tensor_tensor(tmp[:, :], zs[:, t, c], 1.0, zs[:, t, c], ALU.mult,
                                                          ALU.mult, accum_out=ss[:, i:i + 1]))

                weights(0)
                weights(1)
                for n in range(SSD_HEADS):
                    if n + 2 < SSD_HEADS:
                        weights(n + 2)
                    product(n)
                    if n % 4 == 2:
                        dve_split_upto(dve, g0 + n // 4 + 2)
                    if n % 8 in (1, 5) and n > 8:
                        gate(n // 8 - 1, [n % 8 // 4])
                gate(3, range(NT))
                inverse_root(dve, NT * 4, 1.0 / 512)
                for t in range(NT):
                    zv = zs[:, t, :].rearrange("p (g e) -> p g e", g=4)
                    v.tensor_tensor(zv, zv, rs[:, 4 * t:4 * t + 4].unsqueeze(2).broadcast_to([P, 4, 512]),
                                    ALU.mult).then_inc(xn_ready.sem, 1)

            for s in (s_ready, a_ready, e_ready, m_ready, o_ready):
                s.passed(SSD_HEADS)
            group_free.passed(8)
            act_free.passed(10)
            st.slot = g0 + 8

        def route(comb):
            local = ExitStack()
            lg = sb("lg", [P, NT, 36], where=local)
            br = sb("br", [P, 36], where=local)
            em = sb("em", [P, NT, 32], where=local)
            ps = sb("ps", [P, NT, 32], where=local)
            oh = sb("oh", [P, 2, NT, 32], where=local)
            gg = sb("gg", [P, 4, NT, 4], where=local)
            sv = sb("sv", [P, 12, NT], where=local)
            cw = sb("cw", [P, NT, 32], where=local)
            ctr = sb("ctr", [32, T], where=local)
            start = h_new.base

            @block.gpsimd
            def _(pool):
                pool.wait_ge(h_new.sem, start)
                pool.dma_start(br[:, :], rows["route"].partition_broadcast(P).rearrange("p o n -> p (o n)")
                               ).then_inc(phase_in[1].sem, 16)

            project(1, False, lambda j, bank: nc.scalar.activation(lg[:, :, :], bank, ACT.Copy), width=36)
            ready = act_free.base

            @block.vector
            def _(dve):
                v = nc.vector
                dve.wait_ge(act_free.sem, ready)
                dve.wait_ge(phase_in[1].sem, 64)

                def wide(a, n):
                    return a.unsqueeze(2).broadcast_to([P, NT, n])

                def row(c, n):
                    return cst[:, c:c + n].unsqueeze(1).broadcast_to([P, NT, n])

                def one_hot(dst, values, top, c, n, work):
                    vlink(dve, v.tensor_tensor(work, values, wide(top, n), ALU.is_equal))
                    vlink(dve, v.tensor_tensor(work, work, row(c, n), ALU.mult))
                    vlink(dve, v.tensor_reduce(sv[:, 11], work, X, ALU.max))
                    vlink(dve, v.tensor_tensor(dst, work, wide(sv[:, 11], n), ALU.is_equal))

                vlink(dve, v.tensor_tensor(lg[:, :, :], lg[:, :, :], br[:, :].unsqueeze(1).broadcast_to([P, NT, 36]),
                                           ALU.add))
                gl, el = lg[:, :, 0:4], lg[:, :, 4:36]
                vlink(dve, v.tensor_reduce(sv[:, 0], gl, X, ALU.max))
                vlink(dve, v.tensor_tensor(gg[:, 0], gl, wide(sv[:, 0], 4), ALU.subtract))
                one_hot(gg[:, 1], gl, sv[:, 0], C_W4, 4, gg[:, 2])
                vlink(dve, v.tensor_scalar(gg[:, 2], gg[:, 1], -1.0, -NEG, ALU.add, ALU.mult))
                for t in range(NT):
                    ins = v.tensor_tensor(em[:, t, :].rearrange("p (g e) -> p g e", g=4),
                                          el[:, t, :].rearrange("p (g e) -> p g e", g=4),
                                          gg[:, 2, t, :].unsqueeze(2).broadcast_to([P, 4, 8]), ALU.add)
                vlink(dve, ins)
                vlink(dve, v.tensor_reduce(sv[:, 1], em[:, :, :], X, ALU.max))
                one_hot(oh[:, 0], em[:, :, :], sv[:, 1], C_W32, 32, ps[:, :, :])
                vlink(dve, v.scalar_tensor_tensor(em[:, :, :], oh[:, 0], 3.0 * NEG, em[:, :, :], ALU.mult, ALU.add))
                vlink(dve, v.tensor_reduce(sv[:, 2], em[:, :, :], X, ALU.max))
                one_hot(oh[:, 1], em[:, :, :], sv[:, 2], C_W32, 32, ps[:, :, :])
                v.tensor_tensor(sv[:, 3], sv[:, 2], sv[:, 1], ALU.subtract).then_inc(ask.sem, 1)
                dve.wait_ge(side.sem, side.at(1))
                vlink(dve, v.tensor_reduce(sv[:, 5], gg[:, 3], X, ALU.add))
                vlink(dve, v.tensor_scalar(sv[:, 6], sv[:, 4], 1.0, None, ALU.add))
                vlink(dve, v.tensor_tensor(sv[:, 6], sv[:, 6], sv[:, 5], ALU.mult))
                vlink(dve, v.reciprocal(sv[:, 6], sv[:, 6]))
                vlink(dve, v.tensor_tensor(sv[:, 7], sv[:, 6], sv[:, 4], ALU.mult))
                vlink(dve, v.tensor_tensor(oh[:, 0], oh[:, 0], wide(sv[:, 6], 32), ALU.mult))
                vlink(dve, v.tensor_tensor(oh[:, 1], oh[:, 1], wide(sv[:, 7], 32), ALU.mult))
                v.tensor_tensor(cw[:, :, :], oh[:, 0], oh[:, 1], ALU.add).then_inc(a_ready.sem, 1)

            @block.scalar
            def _(act):
                act.wait_ge(ask.sem, ask.at(0))
                nc.scalar.activation(sv[:, 4], sv[:, 3], ACT.Exp).then_inc(side.sem, 1)
                nc.scalar.activation(gg[:, 3], gg[:, 0], ACT.Exp).then_inc(side.sem, 1)
                act.wait_ge(transposed.sem, transposed.at(0))
                nc.scalar.activation(ctr[:, :], A[0:32, 1, 0:T], ACT.Copy).then_inc(side.sem, 1)
                for j in range(EXPERTS // 2):
                    act.wait_ge(o_ready.sem, o_ready.at(j))
                    nc.scalar.activation(comb[:, 2 * j:2 * j + 2, :],
                                         A[:, j % 4, :].rearrange("p (e t) -> p e t", e=2),
                                         ACT.Copy).then_inc(act_free.sem, 1)

            @block.tensor
            def _(pe):
                pe.wait_ge(a_ready.sem, a_ready.at(0))
                for t in range(NT):
                    ins = nc.tensor.transpose(A[0:32, 1, t * P:(t + 1) * P], cw[:, t, :], ident)
                ins.then_inc(transposed.sem, 1)
                pe.wait_ge(side.sem, side.at(2))
                for j in range(EXPERTS // 2):
                    if j >= 4:
                        pe.wait_ge(act_free.sem, act_free.at(j - 4))
                    for q in range(2):
                        e = 2 * j + q
                        ins = nc.tensor.matmul(A[:, j % 4, q * T:(q + 1) * T],
                                               lhsT=cst[0:32, C_ID + e:C_ID + e + 1].broadcast_to([32, P]),
                                               rhs=ctr[:, :], start=True, stop=True)
                    ins.then_inc(o_ready.sem, 1)

            ask.passed(1)
            side.passed(3)
            transposed.passed(1)
            a_ready.passed(1)
            o_ready.passed(EXPERTS // 2)
            act_free.passed(EXPERTS // 2)
            copied = act_free.base

            @block.tensor
            def _(pe):
                pe.wait_ge(act_free.sem, copied)

            @block.vector
            def _(dve):
                dve.wait_ge(act_free.sem, copied)
            local.close()

        def add_y(factor=1.0):
            @block.vector
            def _(dve):
                for t in range(NT):
                    wait_product(dve, t)
                    nc.vector.tensor_tensor(h[:, t, :], h[:, t, :], Y[:, t, :], ALU.add).then_inc(h_new.sem, 1)
            h_new.passed(NT)

        @block.sync
        def _(sp):
            sp.dma_start(h[:, :, :], x_in.rearrange("(t p) d -> p t d", p=P)).then_inc(consts_in.sem, 16)
            sp.dma_start(cst[:, :], const).then_inc(consts_in.sem, 16)
            sp.dma_start(col[:, :], cols).then_inc(consts_in.sem, 16)
            with sp.Fori(0, n_slots // RING) as i:
                for r in range(RING):
                    sp.wait_ge(lo_ready.sem, RING * i + r + 1)
                    sp.dma_start(raw[:, r, :], stream[bass.ds(RING * i + r, 1), :, :]
                                 .rearrange("s p c -> (s p) c")).then_inc(raw_loaded[r].sem, 16)
            for n in range(n_slots // RING * RING, n_slots):
                sp.wait_ge(lo_ready.sem, n + 1)
                sp.dma_start(raw[:, n % RING, :], stream[n, :, :]).then_inc(raw_loaded[n % RING].sem, 16)

        @block.gpsimd
        def _(pool):
            for i in range(2):
                pool.dma_start(gains[:, i, :], rows["post"][i:i + 1, :].partition_broadcast(P)
                               .rearrange("p o d -> p (o d)")).then_inc(gain_in[i].sem, 16)

        @block.vector
        def _(dve):
            nc.vector.memset(zero[:, 0:128].bitcast(F32), 0.0).then_inc(lo_ready.sem, RING)
            nc.vector.memset(zero[:, 128:256].bitcast(F32), 0.0).then_inc(group_free.sem, 1)
            nc.vector.memset(zero[:, 256:512].bitcast(F32), 0.0).then_inc(zero_ready.sem, 1)
            dve.wait_ge(consts_in.sem, 48)

        @block.tensor
        def _(pe):
            pe.wait_ge(consts_in.sem, 48)

        def first_block():
            pre_norm("g00")
            ffn(FF_STEPS)
            post_norm(0.5)
            pre_norm("g02")
            gated_conv()
            post_norm(1.0)
            pre_norm("g04")
            ffn(FF_STEPS)
            post_norm(0.5)
            with ExitStack() as attention:
                kt = sb("kt", [P, KD, T], where=attention)
                vt = sb("vt", [P, NT, D], where=attention)
                pre_norm("kv")
                key_value(kt, vt)
                pre_norm("g10")
                ffn(FF_STEPS)
                post_norm(0.5)
                pre_norm("g12")
                diff_attention(kt, vt)
                post_norm(1.0)
            pre_norm("g14")
            ffn(FF_STEPS)
            post_norm(0.5)

        def second_block():
            with ExitStack() as mixer:
                ya_hi = sb("ya_hi", [P, KD, T], F32R, where=mixer)
                ya_lo = sb("ya_lo", [P, KD, T], F32R, where=mixer)
                iw = sb("iw", [P, NT, IDX_HEADS], where=mixer)
                zs = sb("zs", [P, NT, 2048], where=mixer)
                pre_norm("attn2")
                sparse_attention(ya_hi, ya_lo, iw, zs)
                with ExitStack() as ssd:
                    ga = xn
                    gb = sb("gb", [P, NT, D], where=ssd)
                    with ExitStack() as scan:
                        xs = sb("xs", [P, NT, 2048], where=scan)
                        bt = sb("bt", [P, 4, T], where=scan)
                        ct = sb("ct", [P, 4, T], where=scan)
                        state_space_inputs(xs, bt, ct)
                        state_space(xs, zs, bt, ct, ga, gb, scan)
                    ys_hi = sb("ys_hi", [P, 16, T], F32R, where=ssd)
                    ys_lo = sb("ys_lo", [P, 16, T], F32R, where=ssd)
                    gates = act_free.base
                    rows_product(4, ya_hi, ya_lo, (group_free.sem, group_free.base))

                    @block.tensor
                    def _(pe):
                        pe.wait_ge(act_free.sem, gates)

                    ready = xn_ready.base
                    for k0 in (0, 8):
                        if k0:
                            xn_ready.base = ready
                            done = xt_ready.base

                            @block.tensor
                            def _(pe):
                                pe.wait_ge(xt_ready.sem, done)
                        transpose_split(lambda t, k: zs[:, t, (k0 + k) * P:(k0 + k + 1) * P], COLS["ssd"],
                                        ys_hi, ys_lo, k0)

                    @block.vector
                    def _(dve):
                        dve.wait_ge(act_free.sem, gates)
                        for t in range(NT):
                            wait_product(dve, t)
                            nc.vector.tensor_tensor(xn[:, t, :], ga[:, t, :], Y[:, t, :],
                                                    ALU.mult).then_inc(group_free.sem, 1)
                    group_free.passed(NT)
                    rows_product(8, ys_hi, ys_lo, (group_free.sem, group_free.base))

                    @block.vector
                    def _(dve):
                        for t in range(NT):
                            wait_product(dve, t)
                            vlink(dve, nc.vector.tensor_tensor(gb[:, t, :], gb[:, t, :], Y[:, t, :], ALU.mult))
                            nc.vector.tensor_tensor(xn[:, t, :], xn[:, t, :], gb[:, t, :],
                                                    ALU.add).then_inc(xn_ready.sem, 1)
                    transpose_split(lambda t, k: xn[:, t, k * P:(k + 1) * P], None)
                    rows_product(4, xh, xl)
                    add_y()
            with ExitStack() as moe:
                comb = sb("comb", [P, EXPERTS, T], where=moe)
                pre_norm("ffn2")
                route(comb)
                ffn(EXPERTS, comb)
                add_y()

        first_block()
        second_block()

        @block.sync
        def _(sp):
            for t in range(NT):
                sp.wait_ge(h_new.sem, h_new.base - NT + 1 + t)
                sp.dma_start(out[t * P:(t + 1) * P, :], h[:, t, :]).then_inc(stored.sem, 16)
            sp.wait_ge(stored.sem, 16 * NT)


def column_slots(w, first, count, width=256):
    w = w[:, first:first + count * width].reshape(KD, P, count, width)
    return np.ascontiguousarray(w.transpose(2, 1, 0, 3)).reshape(count, P, KD * width)


def row_slots(w):
    w = w.reshape(-1, 2, P, D)
    return np.ascontiguousarray(w.transpose(0, 2, 1, 3)).reshape(-1, P, 2 * D)


def interleave(gate, up, down):
    parts = [gate[0:1], up[0:1]]
    for s in range(1, len(gate)):
        parts += [gate[s:s + 1], up[s:s + 1], down[s - 1:s]]
    return parts + [down[-1:]]


def padded(parts):
    w = np.concatenate(parts, axis=1)
    return column_slots(np.concatenate([w, np.zeros((D, 256 - w.shape[1]), w.dtype)], axis=1), 0, 1)


def weight_stream(w):
    parts = []

    def ffn(l, i):
        gu, down = w["ffn_w_gu"][l, i], w["ffn_w_down"][l, i]
        parts.extend(interleave(column_slots(gu, 0, FF_STEPS), column_slots(gu, 2816, FF_STEPS), row_slots(down)))

    ffn(0, 0)
    b, c, z = (column_slots(w["conv_w_in"][0], D * i, 4) for i in range(3))
    d = row_slots(w["conv_w_out"][0])
    for j in range(4):
        parts.extend([b[j:j + 1], c[j:j + 1], z[j:j + 1]])
        if j:
            parts.append(d[j - 1:j])
    parts.append(d[3:4])
    ffn(0, 1)
    parts.append(column_slots(w["w_kv"], 0, 4))
    parts.append(row_slots(w["w_kv"][:, D:]))
    ffn(1, 0)
    parts.append(column_slots(w["attn_w_q"][0], 0, 4))
    parts.append(row_slots(w["attn_w_o"][0]))
    ffn(1, 1)
    wi = w["w_in_2"][0]
    parts.append(column_slots(wi, 0, 5))
    parts.append(column_slots(wi, 1536, 2))
    parts.append(column_slots(wi, 1280, 1))
    parts.append(padded([wi[:, 2048:2120], wi[:, 7240:7272]]))
    parts.append(column_slots(wi, 2120, 8))
    parts.append(column_slots(wi, 4168, 12))
    parts.append(column_slots(wi, 7272, 8))
    parts.append(row_slots(w["w_attn_branch_2"][0]))
    parts.append(row_slots(w["w_ssd_branch_2"][0]))
    parts.append(row_slots(w["w_out_2"][0]))
    parts.append(padded([w["w_route_group_2"][0], w["w_route_expert_2"][0]]))
    gate = w["w_gate_2"][0].reshape(EXPERTS, KD, P, 256).transpose(0, 2, 1, 3).reshape(EXPERTS, P, SLOT)
    up = w["w_up_2"][0].reshape(EXPERTS, KD, P, 256).transpose(0, 2, 1, 3).reshape(EXPERTS, P, SLOT)
    down = w["w_down_2"][0].reshape(EXPERTS, 2, P, D).transpose(0, 2, 1, 3).reshape(EXPERTS, P, SLOT)
    parts.extend(interleave(gate, up, down))
    return np.concatenate(parts, axis=0)


def constants():
    i = np.arange(P)
    c = np.zeros((P, N_CONST), np.float32)
    c[:, C_ID:C_ID + P] = np.eye(P)
    tri = (i[:, None] <= i[None, :]).astype(np.float32)
    c[:, C_TRI:C_TRI + P] = tri
    c[:, C_ONE:C_ONE + P] = 1.0
    c[:, C_TRI2:C_TRI2 + P] = tri
    c[:, C_GT:C_GT + P] = i[:, None] > i[None, :]
    inv = np.float32(500000.0) ** (-np.arange(8, dtype=np.float32) * np.float32(2.0) / np.float32(16))
    for t in range(NT):
        ang = (i + t * P).astype(np.float32)[:, None] * inv[None, :]
        c[:, C_COS + 8 * t:C_COS + 8 * t + 8] = np.cos(ang)
        c[:, C_SIN + 8 * t:C_SIN + 8 * t + 8] = np.sin(ang)
    c[:, C_W4:C_W4 + 4] = 4 - np.arange(4)
    c[:, C_W32:C_W32 + 32] = 32 - np.arange(32)
    q = i[:, None] + P * np.arange(NT)[None, :]
    k = np.arange(T)
    kmq = (k[None, None, :] - q[:, :, None]).astype(np.float32)
    attn = np.stack([kmq, np.where(kmq <= 0, 0.0, NEG).astype(np.float32)], axis=1)
    adm = np.where(k[None, None, :] // 64 <= q[:, :, None] // 64, 0.0, NEG).astype(np.float32)
    return c, attn.reshape(P, -1).astype(np.float32), adm.reshape(P, -1)


def feature_columns(w):
    g = w["norm_g"]
    parts = [g[0, 0], g[0, 2], g[0, 4], g[1, 0], g[1, 2], g[1, 4], w["kv_norm_g"], w["conv_k"][0].reshape(-1),
             w["attn_subln_g"][0], w["attn_norm_2"][0], w["ffn_norm_2"][0], w["ssd_norm_2"][0],
             w["conv_w_2"][0].reshape(-1), w["conv_b_2"][0]]
    return np.ascontiguousarray(np.concatenate(parts).reshape(-1, P).T)


def kernel(**inputs):
    import concourse.bacc as bacc
    from concourse.bass_utils import run_bass_kernel_spmd

    w = {k: np.asarray(v) for k, v in inputs.items()}
    const, attn, adm = constants()
    g = w["norm_g"]
    arrays = {
        "stream": weight_stream(w),
        "x_in": w["x"][0],
        "cols": feature_columns(w),
        "const": const,
        "attn_const": attn,
        "adm_const": adm,
        "post_rows": np.stack([g[0, 1], g[0, 3], g[0, 5], g[1, 1], g[1, 3], g[1, 5]]),
        "qk_rows": np.concatenate([w["q_norm_2"], w["k_norm_2"], w["idx_k_norm_2"]]),
        "ssd_rows": np.concatenate([w["dt_bias_2"], w["a_log_2"], w["d_skip_2"]]),
        "route_row": np.concatenate([w["b_route_group_2"], w["b_route_expert_2"]], axis=1),
        "lam": w["attn_lambda"][0],
    }
    nc = bacc.Bacc("TRN2", target_bir_lowering=False, num_devices=1)
    ap = {n: nc.dram_tensor(n, a.shape, mybir.dt.from_np(a.dtype), kind="ExternalInput").ap()
          for n, a in arrays.items()}
    out = nc.dram_tensor("out", (T, D), F32, kind="ExternalOutput").ap()
    rows = {"post": ap["post_rows"], "qk": ap["qk_rows"], "ssd": ap["ssd_rows"], "route": ap["route_row"]}
    build(nc, ap["stream"], ap["x_in"], out, ap["cols"], ap["const"], ap["attn_const"], ap["adm_const"],
          rows, ap["lam"])
    r = run_bass_kernel_spmd(nc, [arrays], core_ids=[0])
    return r.results[0]["out"].reshape(1, T, D)
```
